# Optimizing a Trainium2 kernel written in Bass

```python
import math
import jax, jax.numpy as jnp
from jax import lax
import numpy as np

D_MODEL = 1024
BATCH = 1
SEQ = 256
DEPTH = 2

M_HEADS = 4
M_HEAD_DIM = 64
M_WIDTH = M_HEADS * M_HEAD_DIM
A_HEADS = 8
A_HEAD_DIM = 64
A_WIDTH = A_HEADS * A_HEAD_DIM
S_GROUPS = 16
S_GROUP_DIM = 16
S_WIDTH = S_GROUPS * S_GROUP_DIM
S_STATE = 64
D_MIX = M_WIDTH + A_WIDTH + S_WIDTH

CONV_K = 4
M_CHUNK = 64
MOBA_BLOCK = 256
MOBA_TOPK = 3
MOBA_QCHUNK = 32
ROPE_THETA = 500000.0
ROPE_DIM = A_HEAD_DIM // 4

N_GROUPS = 4
EXPERTS_PER_GROUP = 8
N_EXPERTS = N_GROUPS * EXPERTS_PER_GROUP
EXPERT_TOPK = 2
D_EXPERT = 512
DISPATCH_BLOCK = 128
EPS = 1e-6

COL_SIZES = [M_WIDTH, M_WIDTH, M_WIDTH, M_WIDTH, M_HEADS, M_HEADS,
             A_WIDTH, A_WIDTH, A_WIDTH,
             S_WIDTH]
D_IN = int(sum(COL_SIZES))
COL_SPLITS = [int(c) for c in np.cumsum(COL_SIZES)[:-1]]

kernel_name = "hymba_style_mlstm_moba_s5_hmoe"

F32 = jnp.float32

def rmsnorm(x, g):
    xf = x.astype(F32)
    y = xf * lax.rsqrt(jnp.mean(xf * xf, axis=-1, keepdims=True) + EPS)
    return (y * g.astype(F32)).astype(x.dtype)

def causal_dwconv(x, w, b):
    kw, s = w.shape[0], x.shape[1]
    xp = jnp.pad(x, ((0, 0), (kw - 1, 0), (0, 0)))
    y = b
    for j in range(kw):
        y = y + xp[:, j:j + s] * w[j]
    return y

def partial_rope(x, pos):
    half = ROPE_DIM // 2
    inv = ROPE_THETA ** (-jnp.arange(half, dtype=F32) * 2.0 / ROPE_DIM)
    ang = pos[:, None] * inv[None, :]
    cos, sin = jnp.cos(ang)[:, None, :], jnp.sin(ang)[:, None, :]
    x1 = x[..., :half].astype(F32)
    x2 = x[..., half:ROPE_DIM].astype(F32)
    rot = jnp.concatenate([x1 * cos - x2 * sin, x2 * cos + x1 * sin], axis=-1).astype(x.dtype)
    return jnp.concatenate([rot, x[..., ROPE_DIM:]], axis=-1)

def mlstm_heads(q, k, v, o_pre, i_pre, f_pre, out_g):
    bsz, s, _ = q.shape
    nc = s // M_CHUNK
    dh = M_HEAD_DIM

    def to_chunks(t):
        return t.astype(F32).reshape(bsz, nc, M_CHUNK, M_HEADS, dh).transpose(1, 0, 3, 2, 4)

    def gate_chunks(g):
        return g.astype(F32).reshape(bsz, nc, M_CHUNK, M_HEADS).transpose(1, 0, 3, 2)

    qc, kc, vc = to_chunks(q), to_chunks(k) * (dh ** -0.5), to_chunks(v)
    ic = gate_chunks(i_pre)
    lfc = jax.nn.log_sigmoid(gate_chunks(f_pre))
    causal = jnp.tril(jnp.ones((M_CHUNK, M_CHUNK), dtype=bool))

    def step(carry, inp):
        C, n, m = carry
        qb, kb, vb, ib, lfb = inp
        b = jnp.cumsum(lfb, axis=-1)
        a = b + m[..., None]
        W = b[..., :, None] - b[..., None, :] + ib[..., None, :]
        W = jnp.where(causal, W, -jnp.inf)
        m_t = jnp.maximum(a, jnp.max(W, axis=-1))
        inter = jnp.exp(a - m_t)
        Sqk = jnp.einsum('bhtd,bhsd->bhts', qb, kb) * jnp.exp(W - m_t[..., None])
        num = inter[..., None] * jnp.einsum('bhtd,bhde->bhte', qb, C) + jnp.einsum('bhts,bhse->bhte', Sqk, vb)
        den = inter * jnp.einsum('bhtd,bhd->bht', qb, n) + jnp.sum(Sqk, axis=-1)
        h = num / jnp.maximum(jnp.abs(den), jnp.exp(-m_t))[..., None]
        bL = b[..., -1]
        g_s = bL[..., None] - b + ib
        m_new = jnp.maximum(bL + m, jnp.max(g_s, axis=-1))
        decay = jnp.exp(bL + m - m_new)
        wts = jnp.exp(g_s - m_new[..., None])
        C_new = decay[..., None, None] * C + jnp.einsum('bhs,bhsd,bhse->bhde', wts, kb, vb)
        n_new = decay[..., None] * n + jnp.einsum('bhs,bhsd->bhd', wts, kb)
        return (C_new, n_new, m_new), h

    init = (jnp.zeros((bsz, M_HEADS, dh, dh), F32), jnp.zeros((bsz, M_HEADS, dh), F32),
            jnp.zeros((bsz, M_HEADS), F32))
    _, hs = lax.scan(step, init, (qc, kc, vc, ic, lfc))
    h = hs.transpose(1, 0, 3, 2, 4).reshape(bsz, s, M_HEADS, dh)
    h = rmsnorm(h, out_g).reshape(bsz, s, M_WIDTH)
    return (h * jax.nn.sigmoid(o_pre.astype(F32))).astype(q.dtype)

def moba_heads(q, k, v, q_g, k_g, out_g):
    bsz, s, _ = q.shape
    dh = A_HEAD_DIM
    pos = jnp.arange(s, dtype=F32)
    heads = lambda t: t.reshape(bsz, s, A_HEADS, dh)
    q = partial_rope(rmsnorm(heads(q), q_g), pos).transpose(0, 2, 1, 3)
    k = partial_rope(rmsnorm(heads(k), k_g), pos).transpose(0, 2, 1, 3)
    v = heads(v).transpose(0, 2, 1, 3)
    nb = -(-s // MOBA_BLOCK)
    pad = nb * MOBA_BLOCK - s
    padk = lambda t: jnp.pad(t, ((0, 0), (0, 0), (0, pad), (0, 0))).reshape(bsz, A_HEADS, nb, MOBA_BLOCK, dh)
    kb, vb = padk(k), padk(v)
    q_blk = jnp.arange(s) // MOBA_BLOCK
    gate = jnp.einsum('bhsd,bhnd->bhsn', q, jnp.mean(kb, axis=3)).astype(F32)
    past = jnp.arange(nb)[None, :] < q_blk[:, None]
    gate = jnp.where(past, gate, -jnp.inf)
    n_sel = min(MOBA_TOPK, nb)
    _, sel = lax.top_k(gate, n_sel)
    sel_ok = sel < q_blk[:, None]
    nq = s // MOBA_QCHUNK

    def chunk(t):
        return jnp.moveaxis(t.reshape(t.shape[0], t.shape[1], nq, MOBA_QCHUNK, *t.shape[3:]), 2, 0)

    bi = jnp.arange(bsz)[:, None, None, None]
    hi = jnp.arange(A_HEADS)[None, :, None, None]
    scale = dh ** -0.5

    def attend(args):
        qc, sc, okc, c = args
        start = c * MOBA_QCHUNK
        own = start // MOBA_BLOCK
        ko = lax.dynamic_index_in_dim(kb, own, axis=2, keepdims=False)
        vo = lax.dynamic_index_in_dim(vb, own, axis=2, keepdims=False)
        qpos = start + jnp.arange(MOBA_QCHUNK)
        kpos = own * MOBA_BLOCK + jnp.arange(MOBA_BLOCK)
        s_own = jnp.einsum('bhqd,bhkd->bhqk', qc, ko).astype(F32) * scale
        s_own = jnp.where(kpos[None, :] <= qpos[:, None], s_own, -jnp.inf)
        ks = kb[bi, hi, sc]
        vs = vb[bi, hi, sc]
        s_sel = jnp.einsum('bhqd,bhqnkd->bhqnk', qc, ks).astype(F32) * scale
        s_sel = jnp.where(okc[..., None], s_sel, -jnp.inf)
        logits = jnp.concatenate([s_sel.reshape(bsz, A_HEADS, MOBA_QCHUNK, n_sel * MOBA_BLOCK), s_own], axis=-1)
        p = jax.nn.softmax(logits, axis=-1).astype(v.dtype)
        p_sel = p[..., :n_sel * MOBA_BLOCK].reshape(bsz, A_HEADS, MOBA_QCHUNK, n_sel, MOBA_BLOCK)
        p_own = p[..., n_sel * MOBA_BLOCK:]
        return jnp.einsum('bhqnk,bhqnkd->bhqd', p_sel, vs) + jnp.einsum('bhqk,bhkd->bhqd', p_own, vo)

    out = lax.map(attend, (chunk(q), chunk(sel), chunk(sel_ok), jnp.arange(nq)))
    out = out.transpose(1, 0, 3, 2, 4).reshape(bsz, s, A_HEADS, dh)
    return rmsnorm(out, out_g).reshape(bsz, s, A_WIDTH)

def s5_groups(u, a_re, a_im, b_re, b_im, c_re, c_im, d, log_dt, glu_w, glu_b, out_g):
    bsz, s, _ = u.shape
    ug = u.astype(F32).reshape(bsz, s, S_GROUPS, S_GROUP_DIM)
    lr, li = a_re.astype(F32), a_im.astype(F32)
    dt = jnp.exp(log_dt.astype(F32))[:, None]
    mag = jnp.exp(lr * dt)
    abar_re, abar_im = mag * jnp.cos(li * dt), mag * jnp.sin(li * dt)
    zr, zi = abar_re - 1.0, abar_im
    den = lr * lr + li * li
    fr, fi = (zr * lr + zi * li) / den, (zi * lr - zr * li) / den
    br, bim = b_re.astype(F32), b_im.astype(F32)
    bbar_re = fr[..., None] * br - fi[..., None] * bim
    bbar_im = fr[..., None] * bim + fi[..., None] * br
    bu_re = jnp.einsum('bsgh,gph->bsgp', ug, bbar_re)
    bu_im = jnp.einsum('bsgh,gph->bsgp', ug, bbar_im)
    ar = jnp.broadcast_to(abar_re, bu_re.shape)
    ai = jnp.broadcast_to(abar_im, bu_re.shape)

    def combine(e1, e2):
        a1r, a1i, b1r, b1i = e1
        a2r, a2i, b2r, b2i = e2
        return (a2r * a1r - a2i * a1i, a2r * a1i + a2i * a1r,
                a2r * b1r - a2i * b1i + b2r, a2r * b1i + a2i * b1r + b2i)

    _, _, xr, xi = lax.associative_scan(combine, (ar, ai, bu_re, bu_im), axis=1)
    y = (jnp.einsum('bsgp,ghp->bsgh', xr, c_re.astype(F32))
         - jnp.einsum('bsgp,ghp->bsgh', xi, c_im.astype(F32))
         + d.astype(F32) * ug).reshape(bsz, s, S_WIDTH)
    z = jax.nn.gelu(y)
    y = z * jax.nn.sigmoid(z @ glu_w.astype(F32) + glu_b.astype(F32))
    y = rmsnorm(y.reshape(bsz, s, S_GROUPS, S_GROUP_DIM), out_g).reshape(bsz, s, S_WIDTH)
    return y.astype(u.dtype)

def hierarchical_moe(x, w_group, b_group, w_expert, b_expert, w_gate, w_up, w_down):
    bsz, s, dm = x.shape
    T = bsz * s
    xf = x.reshape(T, dm)
    gl = (xf @ w_group).astype(F32) + b_group.astype(F32)
    pg = jax.nn.softmax(gl, axis=-1)
    g_sel = jnp.argmax(gl, axis=-1)
    el = ((xf @ w_expert).astype(F32) + b_expert.astype(F32)).reshape(T, N_GROUPS, EXPERTS_PER_GROUP)
    el_g = jnp.take_along_axis(el, g_sel[:, None, None], axis=1)[:, 0]
    top_v, top_i = lax.top_k(el_g, EXPERT_TOPK)
    wts = jax.nn.softmax(top_v, axis=-1) * jnp.take_along_axis(pg, g_sel[:, None], axis=1)
    eid = g_sel[:, None] * EXPERTS_PER_GROUP + top_i
    A = T * EXPERT_TOPK
    e_flat = eid.reshape(-1)
    tok_flat = jnp.repeat(jnp.arange(T, dtype=jnp.int32), EXPERT_TOPK)
    w_flat = wts.reshape(-1)
    order = jnp.argsort(e_flat)
    e_s, tok_s, w_s = e_flat[order], tok_flat[order], w_flat[order]
    counts = jnp.bincount(e_flat, length=N_EXPERTS)
    starts = jnp.cumsum(counts) - counts
    padded = (counts + DISPATCH_BLOCK - 1) // DISPATCH_BLOCK * DISPATCH_BLOCK
    pends = jnp.cumsum(padded)
    pstarts = pends - padded
    dest = pstarts[e_s] + (jnp.arange(A) - starts[e_s])
    R = (A + N_EXPERTS * (DISPATCH_BLOCK - 1) + DISPATCH_BLOCK - 1) // DISPATCH_BLOCK * DISPATCH_BLOCK
    nblk = R // DISPATCH_BLOCK
    row_tok = jnp.full((R,), T, dtype=jnp.int32).at[dest].set(tok_s)
    row_w = jnp.zeros((R,), F32).at[dest].set(w_s)
    blk_exp = jnp.minimum(jnp.searchsorted(pends, jnp.arange(nblk) * DISPATCH_BLOCK, side='right'),
                          N_EXPERTS - 1)
    x_pad = jnp.concatenate([xf, jnp.zeros((1, dm), xf.dtype)], axis=0)
    xs = x_pad[row_tok].reshape(nblk, DISPATCH_BLOCK, dm)

    def expert_block(args):
        xb, e = args
        h = jax.nn.silu(xb @ w_gate[e]) * (xb @ w_up[e])
        return h @ w_down[e]

    ys = lax.map(expert_block, (xs, blk_exp)).reshape(R, dm)
    out = jax.ops.segment_sum(ys * row_w[:, None].astype(ys.dtype), row_tok, num_segments=T + 1)[:T]
    return out.reshape(bsz, s, dm)

def setup_inputs(seed: int = 0) -> dict:
    key = jax.random.key(seed)
    ks = iter(jax.random.split(key, 64))
    L = DEPTH

    def nrm(shape, scale):
        return jax.random.normal(next(ks), shape, F32) * scale

    def gain(shape):
        return 1.0 + nrm(shape, 0.02)

    x = nrm((BATCH, SEQ, D_MODEL), 1.0)
    s_a_re = -0.5 + nrm((L, S_GROUPS, S_STATE), 0.01)
    s_a_im = math.pi * jnp.arange(S_STATE, dtype=F32)[None, None, :] + nrm((L, S_GROUPS, S_STATE), 0.01)
    log_dt = jnp.log(0.001) + jax.random.uniform(next(ks), (L, S_GROUPS), F32) * (jnp.log(0.1) - jnp.log(0.001))
    cplx_b = S_GROUP_DIM ** -0.5 / math.sqrt(2.0)
    cplx_c = S_STATE ** -0.5 / math.sqrt(2.0)
    return {
        "x": x,
        "norm1_g": gain((L, D_MODEL)),
        "w_in": nrm((L, D_MODEL, D_IN), D_MODEL ** -0.5),
        "m_bias_i": nrm((L, M_HEADS), 0.1),
        "m_bias_f": jnp.linspace(3.0, 6.0, M_HEADS)[None, :] + nrm((L, M_HEADS), 0.1),
        "m_conv_w": nrm((L, CONV_K, 2 * M_WIDTH), CONV_K ** -0.5),
        "m_conv_b": nrm((L, 2 * M_WIDTH), 0.02),
        "m_out_g": gain((L, M_HEADS, M_HEAD_DIM)),
        "a_q_g": gain((L, A_HEAD_DIM)),
        "a_k_g": gain((L, A_HEAD_DIM)),
        "a_out_g": gain((L, A_HEADS, A_HEAD_DIM)),
        "s_a_re": s_a_re,
        "s_a_im": s_a_im,
        "s_b_re": nrm((L, S_GROUPS, S_STATE, S_GROUP_DIM), cplx_b),
        "s_b_im": nrm((L, S_GROUPS, S_STATE, S_GROUP_DIM), cplx_b),
        "s_c_re": nrm((L, S_GROUPS, S_GROUP_DIM, S_STATE), cplx_c),
        "s_c_im": nrm((L, S_GROUPS, S_GROUP_DIM, S_STATE), cplx_c),
        "s_d": nrm((L, S_GROUPS, S_GROUP_DIM), 1.0),
        "s_log_dt": log_dt,
        "s_glu_w": nrm((L, S_WIDTH, S_WIDTH), S_WIDTH ** -0.5),
        "s_glu_b": nrm((L, S_WIDTH), 0.02),
        "s_out_g": gain((L, S_GROUPS, S_GROUP_DIM)),
        "w_out": nrm((L, D_MIX, D_MODEL), D_MIX ** -0.5),
        "norm2_g": gain((L, D_MODEL)),
        "r_group_w": nrm((L, D_MODEL, N_GROUPS), D_MODEL ** -0.5),
        "r_group_b": nrm((L, N_GROUPS), 0.01),
        "r_expert_w": nrm((L, D_MODEL, N_EXPERTS), D_MODEL ** -0.5),
        "r_expert_b": nrm((L, N_EXPERTS), 0.01),
        "e_w_gate": nrm((L, N_EXPERTS, D_MODEL, D_EXPERT), D_MODEL ** -0.5),
        "e_w_up": nrm((L, N_EXPERTS, D_MODEL, D_EXPERT), D_MODEL ** -0.5),
        "e_w_down": nrm((L, N_EXPERTS, D_EXPERT, D_MODEL), D_EXPERT ** -0.5),
    }

def reference(x, norm1_g, w_in, m_bias_i, m_bias_f, m_conv_w, m_conv_b, m_out_g,
              a_q_g, a_k_g, a_out_g, s_a_re, s_a_im, s_b_re, s_b_im, s_c_re, s_c_im,
              s_d, s_log_dt, s_glu_w, s_glu_b, s_out_g, w_out, norm2_g,
              r_group_w, r_group_b, r_expert_w, r_expert_b, e_w_gate, e_w_up, e_w_down):
    for l in range(DEPTH):
        h = rmsnorm(x, norm1_g[l])
        proj = h @ w_in[l]
        mq, mk, mv, mo, mi, mf, aq, ak, av, su = jnp.split(proj, COL_SPLITS, axis=-1)
        qk = jax.nn.silu(causal_dwconv(jnp.concatenate([mq, mk], axis=-1), m_conv_w[l], m_conv_b[l]))
        mq, mk = qk[..., :M_WIDTH], qk[..., M_WIDTH:]
        y_m = mlstm_heads(mq, mk, mv, mo, mi + m_bias_i[l], mf + m_bias_f[l], m_out_g[l])
        y_a = moba_heads(aq, ak, av, a_q_g[l], a_k_g[l], a_out_g[l])
        y_s = s5_groups(su, s_a_re[l], s_a_im[l], s_b_re[l], s_b_im[l], s_c_re[l], s_c_im[l],
                        s_d[l].reshape(S_GROUPS, S_GROUP_DIM), s_log_dt[l], s_glu_w[l], s_glu_b[l], s_out_g[l])
        mix = jnp.concatenate([y_m.astype(x.dtype), y_a.astype(x.dtype), y_s.astype(x.dtype)], axis=-1)
        x = x + mix @ w_out[l]
        x = x + hierarchical_moe(rmsnorm(x, norm2_g[l]), r_group_w[l], r_group_b[l], r_expert_w[l],
                                 r_expert_b[l], e_w_gate[l], e_w_up[l], e_w_down[l])
    return x


_drawn_inputs = setup_inputs


def setup_inputs(seed=0):
    import zlib

    import numpy as np

    out = dict(_drawn_inputs(seed))
    spreads = {}
    factors = {'m_bias_i': 8.0,
     'm_conv_b': 3.835,
     'm_out_g': 4.734,
     'a_q_g': 3.277,
     'a_k_g': 2.962,
     's_a_re': 8.0,
     's_glu_b': 7.865,
     'r_group_b': 4.04,
     'r_expert_b': 3.228}
    for name, (base, spread) in spreads.items():
        noise = np.random.default_rng([zlib.crc32(name.encode()), seed]).standard_normal(out[name].shape)
        drawn = base * np.exp(spread * noise) if base else spread * noise
        out[name] = __import__('jax').numpy.asarray(drawn.astype(out[name].dtype))
    for name, factor in factors.items():
        out[name] = (out[name] * factor).astype(out[name].dtype)
    return out
```

```python
from contextlib import ExitStack

import numpy as np

import concourse.bass as bass
from concourse import mybir

L = 2
T = 256
D = 1024
P = 128
NT = T // P
KD = D // P
DIN = 2824
MH, AH, HD = 4, 8, 64
SG, SH, SS = 16, 16, 64
ST = SG * SS // P
NE, DE = 32, 512
KF = DE // P
EG = 4
CAP = P // EG
NG = NE // EG
MAXU = 16
EPS = 1e-6
BIG = 1e6
NEG = -1e30
TURN = 6.283185
ROUND = 12582912.0
GRID = 3072.0

F32 = mybir.dt.float32
I32 = mybir.dt.int32
U32 = mybir.dt.uint32
ALU = mybir.AluOpType
ACT = mybir.ActivationFunctionType
X = mybir.AxisListType.X

C_IDENT = 0
C_MQK = 128
C_BEFORE = 256
C_ONES = 384
C_BLK = 512
C_CMASK = 640
C_T = 768
C_COS = C_T + T
C_SIN = C_COS + NT * 8
C_SEL = C_SIN + NT * 8
C_GID = C_SEL + MH * P
C_P = C_GID + NE
C_EPS = C_P + 1
C_MHALF = C_EPS + 1
NC = C_MHALF + 2

R_CW, R_CB, R_MG, R_AG, R_SG, R_SD, R_GB, R_LR, R_LI, R_DT = 0, 16, 20, 22, 26, 28, 30, 32, 40, 48
NR = 56


def constants():
    c = np.zeros((P, NC), np.float32)
    p = np.arange(P)
    c[:, C_IDENT:C_IDENT + P] = np.eye(P)
    c[:, C_MQK:C_MQK + P] = np.where(p[None, :] <= p[:, None], 0, NEG)
    c[:, C_BEFORE:C_BEFORE + P] = p[:, None] < p[None, :]
    c[:, C_ONES:C_ONES + P] = 1
    c[:, C_BLK:C_BLK + P] = (p[:, None] // SH == p[None, :] // SH) / SH
    c[:, C_CMASK:C_CMASK + P] = (p[:, None] // SH) % 2 == p[None, :] // SS
    c[:, C_T:C_T + T] = np.arange(T)
    inv = (500000.0 ** (-np.arange(8, dtype=np.float32) * np.float32(2.0) / np.float32(16))).astype(np.float32)
    for j in range(NT):
        ang = (j * P + p).astype(np.float32)[:, None] * inv[None, :]
        c[:, C_COS + 8 * j:C_COS + 8 * j + 8] = np.cos(ang)
        c[:, C_SIN + 8 * j:C_SIN + 8 * j + 8] = np.sin(ang)
    for h in range(MH):
        c[h, C_SEL + P * h:C_SEL + P * h + P] = 1
    c[:, C_GID:C_GID + NE] = np.arange(NE) // 8
    c[:, C_P] = p
    c[:, C_EPS] = EPS
    c[:, C_MHALF:C_MHALF + 2] = -0.5
    return c


def build(nc, out, consts, x, norm1_g, w_in, m_bias_i, m_bias_f, m_conv_w, m_conv_b, m_out_g, a_q_g, a_k_g, a_out_g,
          s_a_re, s_a_im, s_b_re, s_b_im, s_c_re, s_c_im, s_d, s_log_dt, s_glu_w, s_glu_b, s_out_g, w_out, norm2_g,
          r_group_w, r_group_b, r_expert_w, r_expert_b, e_w_gate, e_w_up, e_w_down):
    with ExitStack() as ctx:
        def sb(name, shape, dt=F32):
            return ctx.enter_context(nc.sbuf_tensor(name, shape, dt))

        def sem(name):
            return ctx.enter_context(nc.semaphore(name))

        ring = sb("ring", [P, 3, 8192])
        flat = ring[:, :, :].rearrange("p q n -> p (q n)")
        cst = sb("cst", [P, NC])
        xres = sb("xres", [P, NT, D])
        xs = sb("xs", [P, NT, D])
        hT = sb("hT", [P, KD, T])
        mixT = sb("mixT", [P, KD, T])
        rows = sb("rows", [R_DT, P])
        ldt = sb("ldt", [ST, 2 + P])
        pc = sb("pc", [P, NR])
        qkg = sb("qkg", [P, 2, HD])
        rw = sb("rw", [P, KD, 36])
        rb = sb("rb", [P, 36])
        gluw = sb("gluw", [P, 2, T])
        bc = sb("bc", [P, 2, 2, P])
        bi = sb("bi", [MH, 2])
        qk = sb("qk", [P, NT, 2, 512])
        qkT = sb("qkT", [P, 2, 4, T])
        av = sb("av", [P, NT, 512])
        scr = sb("scr", [P, 1024])
        conv = sb("conv", [P, 4, T + 3])
        qkm = sb("qkm", [P, 4, T])
        vm = sb("vm", [P, NT, T])
        so = sb("so", [P, NT, T])
        tab = sb("tab", [P, 2, ST, T])
        uT = sb("uT", [P, 2, T])
        bT = sb("bT", [P, 4, P])
        cT = sb("cT", [P, 4, P])
        gr = sb("gr", [MH, 6, T])
        small = sb("small", [P, 264])
        ctl = sb("ctl", [1, 2 + MAXU], I32)
        before = sb("before", [1, 2])
        idx = sb("idx", [P, 2, NT, 8], U32)

        gain = av[:, :, :].rearrange("p a n -> p (a n)")
        bmat = bc[:, 0, :, :].rearrange("p r (i h) -> p r i h", h=SH)
        cmat = bc[:, 1, :, :].rearrange("p r (c s) -> p r c s", s=SS)
        pm = mixT[:, 2:4, :].rearrange("p c n -> p (c n)")[:, 0:384]
        dec = conv[:, :, :].rearrange("p c n -> p (c n)")[:, 0:768].rearrange("p (b n) -> p b n", b=2)
        rnd = mixT[:, 0:4, :]
        bu = xs[:, 0, :].rearrange("p (b c t) -> p b c t", b=2, c=2)
        zz = xs[:, 1, :].rearrange("p (b c t) -> p b c t", b=2, c=2)
        ptmp = mixT[:, 6:8, :]
        prob = hT[:, 0:4, :].rearrange("p (b a) t -> p b (a t)", b=2)
        probT = hT[:, 4:8, :].rearrange("p (b a) t -> p b (a t)", b=2)
        xTe = qkT[:, 0, :, :].rearrange("p a t -> p (a t)")
        Y = qkT[:, 1, :, :].rearrange("p a t -> p (a t)")
        hit = qk[:, 0, 0, :].rearrange("p (a j s) -> p a j s", a=2, j=NT)
        hitw = hit[:, 1, :, :]
        hit2 = qk[:, 0, 1, 0:256].rearrange("p (j s) -> p j s", j=NT)
        hitT = qk[:, 0, 1, 256:512].rearrange("p (j t) -> p j t", j=NT)
        es = qk[:, 1, 0, :]
        hx = qk[:, 1, 1, :]
        hTe = scr[:, 0:512]
        rt = so[:, :, :].rearrange("p j n -> p (j n)")
        rv = vm[:, :, :].rearrange("p j n -> p (j n)")

        PS = ctx.enter_context(nc.psum_tensor("PS", [P, 8, 512], F32))
        ident = cst[:, C_IDENT:C_IDENT + P]
        ones = cst[:, C_ONES:C_ONES + P]
        eps = cst[:, C_EPS:C_EPS + 1]

        s_cst = sem("constants_in")
        s_x = sem("x_in")
        s_gain = [sem(f"gain_in_{i + 1}") for i in range(2)]
        s_par = sem("small_weights_in")
        NPAR = 23
        s_win = [sem(f"w_in_{c}") for c in range(6)]
        s_wo = sem("w_out_in")
        s_q = [sem(f"quarter_in_{q}") for q in range(3)]
        s_ow = [sem(f"unit_weights_in_{c}") for c in range(3)]
        s_pj = sem("projected")
        s_sub = sem("sub_used")
        s_ou = [sem(f"unit_weights_used_{c}") for c in range(3)]
        s_ss = sem("square_sums")
        s_rs = sem("row_scales")
        s_xs = sem("xs_ready")
        s_xT = sem("xs_turned")
        s_hTv = sem("hT_by_vector")
        s_hTa = sem("hT_by_scalar")
        s_dr = sem("log_steps_spread")
        s_pcp = sem("columns_turned")
        s_pc = sem("columns_ready")
        s_cm = sem("C_masked")
        s_cTp = sem("C_turned")
        s_cT = sem("CT_ready")
        s_bb = sem("B_discrete")
        s_bTp = sem("B_turned")
        s_bT = sem("BT_ready")
        s_dt = sem("steps_exponent")
        s_lr = sem("decay_exponents")
        s_mag = sem("decays_ready")
        s_phi = sem("turns_ready")
        s_fracv = sem("phases_by_vector")
        s_frac = sem("phases_by_gpsimd")
        s_tab = sem("tables_ready")
        s_uT = sem("uT_ready")
        s_cv = sem("conv_filled")
        s_cvz = sem("conv_zeros")
        s_cy = sem("conv_done")
        s_ce = sem("conv_exp")
        s_qkm = sem("mqk_ready")
        s_vm = sem("v_ready")
        s_oe = sem("o_exp")
        s_aq = sem("aqk_copied")
        s_av = sem("av_ready")
        s_gf = sem("gate_f")
        s_gl = sem("gate_log")
        s_gm = sem("gate_rows")
        s_gTp = sem("gates_turned")
        s_gT = sem("gates_token_major")
        s_fl = sem("floors_ready")
        s_dp = sem("decay_scores")
        s_de = sem("decay_exp")
        s_sp = sem("m_scores")
        s_pm = sem("m_weights")
        s_np = sem("m_numerators")
        s_msq = sem("m_squares")
        s_mrs = sem("m_scales")
        s_hm = sem("m_heads_ready")
        s_hmT = sem("m_heads_turned")
        s_mixm = sem("m_mixed")
        s_qn = sem("qk_squares")
        s_qr = sem("qk_scales")
        s_qkn = sem("qk_normed")
        s_qTp = sem("qk_turned")
        s_qT = sem("qkT_ready")
        s_as = sem("a_scores")
        s_mx = sem("a_maxima")
        s_pr = sem("a_probs")
        s_pTp = sem("a_probs_turned")
        s_pT = sem("a_probsT_ready")
        s_pv = sem("a_values")
        s_osq = sem("a_squares")
        s_ors = sem("a_scales")
        s_on = sem("a_heads_ready")
        s_onT = sem("a_heads_turned")
        s_mixa = sem("a_mixed")
        s_bup = sem("bu_product")
        s_bu = sem("bu_copied")
        s_wi = sem("w_im")
        s_zi = sem("z_scanned")
        s_xr = sem("state_re")
        s_xi = sem("state_im")
        s_y = sem("y_product")
        s_ge = sem("gelu_argument")
        s_gx = sem("gelu_exp")
        s_z = sem("z_ready")
        s_glu = sem("glu_product")
        s_glx = sem("glu_exp")
        s_ysq = sem("y_squares")
        s_ym = sem("y_means")
        s_yr = sem("y_scales")
        s_mixs = sem("s_mixed")
        s_op = sem("out_product")
        s_rp = sem("router_logits")
        s_rg = sem("router_group")
        s_rge = sem("router_group_exp")
        s_rv = sem("router_top")
        s_rve = sem("router_top_exp")
        s_mk = sem("masks_ready")
        s_rk = sem("ranks_ready")
        s_eu = sem("unit_experts")
        s_eup = sem("unit_experts_row")
        s_ctl = sem("units_ready")
        s_xf = sem("x_final")
        s_out = sem("stored")

        class Slots:

            def __init__(self, k, used):
                self.gate, self.up, self.down = used
                self.hit = sem(f"{k}_hits_ready")
                self.gath = sem(f"{k}_gathered")
                self.wt = sem(f"{k}_hits_turned")
                self.wpt = sem(f"{k}_hitsT_ready")
                self.xte = sem(f"{k}_xT_ready")
                self.eg = sem(f"{k}_gate_exp")
                self.h = sem(f"{k}_h_ready")
                self.hps = sem(f"{k}_h_turned")
                self.hte = sem(f"{k}_hT_ready")
                self.ys = sem(f"{k}_y_copied")
                self.comb = sem(f"{k}_combined")

        G = Slots("g", [(s_sub, 6, 2), (s_sub, 6, 4), (s_sub, 6, 6)])
        U = Slots("u", [(s, 1, 2) for s in s_ou])

        def wait_product(eng, product, n):
            s, per, c = product
            eng.wait_ge(s, n * per + c)

        def sc(o, n=ST):
            return small[:, o:o + n]

        ss, rs = sc(0, 2), sc(2, 2)
        mag, phih, phil, dtc, fr, fi, den, t0, t1 = (sc(8 + 8 * i) for i in range(9))
        emt = small[:, 80:88].rearrange("p (j h) -> p j h", j=NT)
        aT = small[:, 88:104].rearrange("p (j w h) -> p j w h", j=NT, w=2)
        mden = small[:, 104:112].rearrange("p (j h) -> p j h", j=NT)
        mss = small[:, 112:120].rearrange("p (j h) -> p j h", j=NT)
        qss = small[:, 120:152].rearrange("p (j a h) -> p j a h", j=NT, a=2)
        amx = small[:, 152:168].rearrange("p (j h) -> p j h", j=NT)
        ars = small[:, 168:184].rearrange("p (j h) -> p j h", j=NT)
        oss = small[:, 184:200].rearrange("p (j h) -> p j h", j=NT)
        ngb = sc(200, 2)

        lg = rt[:, 0:72].rearrange("p (j n) -> p j n", j=NT)
        gl8 = rt[:, 72:88].rearrange("p (j n) -> p j n", j=NT)
        gmx = rt[:, 88:104].rearrange("p (j n) -> p j n", j=NT)
        emx = rt[:, 104:120].rearrange("p (j n) -> p j n", j=NT)
        gsel = rt[:, 120:122].rearrange("p (j n) -> p j n", j=NT)
        pex = rt[:, 122:130].rearrange("p (j n) -> p j n", j=NT)
        pgs = rt[:, 130:132].rearrange("p (j n) -> p j n", j=NT)
        eid = rt[:, 132:136].rearrange("p (j n) -> p j n", j=NT)
        wgt = rt[:, 136:140].rearrange("p (j n) -> p j n", j=NT)
        dif = rt[:, 140:142].rearrange("p (j n) -> p j n", j=NT)
        rkk = rt[:, 142:146].rearrange("p (j n) -> p j n", j=NT)
        usk = rt[:, 146:150].rearrange("p (j n) -> p j n", j=NT)
        far = rt[:, 150:154].rearrange("p (j n) -> p j n", j=NT)
        sg = rt[:, 154:158].rearrange("p (j n) -> p j n", j=NT)
        su = rt[:, 158:162].rearrange("p (j n) -> p j n", j=NT)
        euc = rt[:, 162:163]
        one1 = rt[0:1, 163:164]
        elp = rt[:, 192:256].rearrange("p (j n) -> p j n", j=NT)
        mk = rt[:, 256:384].rearrange("p (a j n) -> p a j n", a=2, j=NT)
        mks = rt[:, 384:448].rearrange("p (j n) -> p j n", j=NT)
        rnk = rv[:, 0:64].rearrange("p (j n) -> p j n", j=NT)
        cnt = rv[:, 64:96]
        nu = rv[:, 96:128]
        uend = rv[:, 128:160]
        ust = rv[:, 160:192]
        rtm = rv[:, 192:256].rearrange("p (j n) -> p j n", j=NT)
        cmp_ = rv[:, 256:288]

        x_v = x.rearrange("b (j p) d -> p (b j) d", p=P)
        out_v = out.rearrange("b (j p) d -> p (b j) d", p=P)
        win_v = w_in.rearrange("l (p k) n -> l p k n", k=KD)
        wo_v = w_out.rearrange("l (k p) n -> l p k n", p=P)
        we_v = [w.rearrange("l e (p k) f -> (l e) p (k f)", p=P) for w in (e_w_gate, e_w_up, e_w_down)]
        CH = [[(2568, 256), (1024, 8)], [(0, 512)], [(512, 512)], [(1032, 512)], [(1544, 512)], [(2056, 512)]]

        def wchunk(c):
            w = sum(n for _, n in CH[c])
            return flat[:, 4096 * c:4096 * c + KD * w].rearrange("p (k n) -> p k n", k=KD)

        wout = ring[:, 0, :].rearrange("p (k n) -> p k n", k=KD)

        def at(ap, l):
            return ap[bass.ds(l, 1)]

        block = ctx.enter_context(nc.Block())

        def wait_apart(eng, s, value):
            value = eng.to_reg(value)
            eng.wait_ge(s_cst, 16)
            eng.wait_ge(s, value)

        QK_BANK = (1, 2, 3, 1)

        def unit(u):
            if u < 2:
                return 0, P, range(u, AH, 2)
            h0 = (0, 4, 1, 5)[u - 2]
            return 1, T, range(h0, h0 + 3, 2)

        def load_small(eng, l):
            eng.dma_start(gain, at(norm1_g, l)[0:1, :].broadcast_to([P, D])).then_inc(s_gain[0], 16)
            n = 0

            def par(dst, src):
                nonlocal n
                n += 1
                eng.dma_start(dst, src).then_inc(s_par, 16)

            def row(r, src, k):
                par(rows[r:r + k, :], src)

            row(R_LR, at(s_a_re, l).rearrange("l (i a) s -> (l i) (a s)", a=2), ST)
            row(R_LI, at(s_a_im, l).rearrange("l (i a) s -> (l i) (a s)", a=2), ST)
            par(ldt[:, 0:2], at(s_log_dt, l).rearrange("l (i a) -> (l i) a", a=2))
            row(R_CW, at(m_conv_w, l).rearrange("l j (c p) -> (l j c) p", p=P), 16)
            row(R_CB, at(m_conv_b, l).rearrange("l (c p) -> (l c) p", p=P), 4)
            row(R_MG, at(m_out_g, l).rearrange("l (c h) d -> (l c) (h d)", h=2), 2)
            row(R_AG, at(a_out_g, l).rearrange("l (c h) d -> (l c) (h d)", h=2), 4)
            row(R_SG, at(s_out_g, l).rearrange("l (c h) d -> (l c) (h d)", h=8), 2)
            row(R_SD, at(s_d, l).rearrange("l (c h) d -> (l c) (h d)", h=8), 2)
            row(R_GB, at(s_glu_b, l).rearrange("l (c p) -> (l c) p", p=P), 2)
            for r, (b, c) in enumerate(((s_b_re, s_c_re), (s_b_im, s_c_im))):
                par(bmat[:, r], at(b, l).rearrange("l (i a) s h -> (l a s) i h", a=2))
                par(cmat[:, r], at(c, l).rearrange("l (c g) h s -> (l g h) c s", c=2))
            par(gluw[:, :, :], at(s_glu_w, l).rearrange("l (c p) n -> (l p) c n", p=P))
            par(bi[:, 0:1], at(m_bias_i, l).rearrange("l h -> h l"))
            par(bi[:, 1:2], at(m_bias_f, l).rearrange("l h -> h l"))
            par(qkg[:, 0, :], at(a_q_g, l).broadcast_to([P, HD]))
            par(qkg[:, 1, :], at(a_k_g, l).broadcast_to([P, HD]))
            par(rw[:, :, 0:4], at(r_group_w, l).rearrange("l (p k) n -> (l p) k n", k=KD))
            par(rw[:, :, 4:36], at(r_expert_w, l).rearrange("l (p k) n -> (l p) k n", k=KD))
            par(rb[:, 0:4], at(r_group_b, l).broadcast_to([P, 4]))
            par(rb[:, 4:36], at(r_expert_b, l).broadcast_to([P, NE]))
            assert n == NPAR, n

        @block.sync
        def _(sp):
            def load_sub(kind, half, quarter, e0):
                src = we_v[kind][bass.ds(e0, EG), :, half * 2048:half * 2048 + 2048].rearrange("e p n -> p e n")
                sp.dma_start(ring[:, quarter, :].rearrange("p (e n) -> p e n", e=EG), src).then_inc(s_q[quarter], 16)

            def load_chunk(c, l):
                a = 0
                for c0, n in CH[c]:
                    sp.dma_start(wchunk(c)[:, :, a:a + n], at(win_v, l)[0, :, :, c0:c0 + n]).then_inc(s_win[c], 16)
                    a += n

            load_small(sp, 0)
            for c in range(6):
                load_chunk(c, 0)
            def layer(l, last):
                wait_apart(sp, s_pj, 12 * l + 4)
                sp.dma_start(wout, at(wo_v, l)[0]).then_inc(s_wo, 16)
                wait_apart(sp, s_pj, 12 * l + 8)
                load_sub(0, 0, 1, l * NE)
                wait_apart(sp, s_pj, 12 * l + 12)
                load_sub(0, 1, 2, l * NE)
                wait_apart(sp, s_op, 2 * l + 2)
                load_sub(1, 0, 0, l * NE)
                if not last:
                    wait_apart(sp, s_ctl, l + 1)
                    load_small(sp, l + 1)
                with sp.Fori(0, NG - 1) as g:
                    for q in range(3, 9):
                        wait_apart(sp, s_sub, l * (6 * NG) + g * 6 + (q - 2))
                        load_sub(q % 6 // 2, q % 2, (q + 1) % 3, l * NE + g * EG + (EG if q >= 6 else 0))
                for q in range(3, 6):
                    wait_apart(sp, s_sub, l * (6 * NG) + (6 * (NG - 1) + q - 2))
                    load_sub(q // 2, q % 2, (q + 1) % 3, l * NE + (NG - 1) * EG)
                wait_apart(sp, s_ctl, l + 1)
                n_u = sp.value_load(ctl[0:1, 0:1], min_val=1, max_val=MAXU - 1)
                u_0 = sp.value_load(ctl[0:1, 1:2], min_val=0, max_val=L * (MAXU - 1))
                wait_apart(sp, s_sub, l * (6 * NG) + (6 * NG - 1))
                with sp.Fori(0, n_u) as u:
                    e = sp.value_load(ctl[0:1, bass.ds(u + 2, 1)], min_val=0, max_val=NE - 1)
                    for kind in range(3):
                        wait_apart(sp, s_ou[kind], u_0 + u + 1)
                        sp.dma_start(flat[:, 4096 * (2 + kind):4096 * (3 + kind)],
                                     we_v[kind][bass.ds(l * NE + e, 1)][0]).then_inc(s_ow[kind], 16)
                if not last:
                    wait_apart(sp, s_sub, l * (6 * NG) + 6 * NG)
                    for c in (0, 1, 5):
                        load_chunk(c, l + 1)
                    for kind in range(3):
                        wait_apart(sp, s_ou[kind], u_0 + n_u + 1)
                        load_chunk(2 + kind, l + 1)

            with sp.Fori(0, L - 1) as l:
                layer(l, False)
            layer(L - 1, True)
            sp.wait_ge(s_xf, L + 1)
            sp.dma_start(out_v, xres[:, :, :]).then_inc(s_out, 16)
            sp.wait_ge(s_out, 16)

        def phases(eng, hf, tmp):
            r = slice(4 * hf, 4 * hf + 4)
            tt = cst[:, C_T:C_T + T].unsqueeze(1).broadcast_to([P, 4, T])
            s, c = tab[:, 1, r, :], tab[:, 0, r, :]
            eng.tensor_tensor(s, tt, phih[:, r].unsqueeze(2).broadcast_to([P, 4, T]), ALU.mult)
            eng.drain()
            eng.tensor_scalar(c, s, ROUND, -ROUND, ALU.add, ALU.add)
            eng.drain()
            eng.tensor_tensor(s, s, c, ALU.subtract)
            eng.tensor_tensor(tmp, tt, phil[:, r].unsqueeze(2).broadcast_to([P, 4, T]), ALU.mult)
            eng.drain()
            eng.tensor_tensor(s, s, tmp, ALU.add)
            eng.drain()
            eng.tensor_scalar(c, s, ROUND, -ROUND, ALU.add, ALU.add)
            eng.drain()
            eng.tensor_tensor(s, s, c, ALU.subtract)
            eng.drain()
            eng.tensor_scalar(c, s, 0.25, None, ALU.add)
            eng.drain()
            eng.tensor_scalar(tmp, c, ROUND, -ROUND, ALU.add, ALU.add)
            eng.drain()
            return eng.tensor_tensor(c, c, tmp, ALU.subtract)

        @block.gpsimd
        def _(pool):
            pool.wait_ge(s_cst, 16)

            def rsqrt_rows(n):
                pool.wait_ge(s_ss, n + 1)
                pool.tensor_tensor(rs, ss, cst[:, C_MHALF:C_MHALF + 2], ALU.pow).then_inc(s_rs, 1)

            with pool.Fori(0, L) as l:
                rsqrt_rows(2 * l)

                pool.wait_ge(s_phi, l + 1)
                phases(pool, 1, rnd).then_inc(s_frac, 1)

                def turn_in(i):
                    b = i % 2
                    pool.wait_ge(s_bu, ST * l + (i + 1))
                    if i >= 2:
                        pool.wait_ge(s_xr, ST * l + (i - 1))
                    pool.tensor_tensor(ptmp[:, 0, :], tab[:, 0, i, :], bu[:, b, 1, :], ALU.mult)
                    pool.tensor_tensor(ptmp[:, 1, :], tab[:, 1, i, :], bu[:, b, 0, :], ALU.mult)
                    pool.drain()
                    pool.tensor_tensor(zz[:, b, 1, :], ptmp[:, 0, :], ptmp[:, 1, :], ALU.subtract).then_inc(s_wi, 1)
                    pool.drain()

                def turn_out(i):
                    b = i % 2
                    pool.wait_ge(s_zi, ST * l + (i + 1))
                    pool.tensor_tensor(ptmp[:, 0, :], tab[:, 1, i, :], zz[:, b, 0, :], ALU.mult)
                    pool.tensor_tensor(ptmp[:, 1, :], tab[:, 0, i, :], zz[:, b, 1, :], ALU.mult)
                    pool.drain()
                    pool.tensor_tensor(bu[:, b, 1, :], ptmp[:, 0, :], ptmp[:, 1, :], ALU.add).then_inc(s_xi, 1)
                    pool.drain()

                pool.wait_ge(s_tab, 2 * l + 1)
                turn_in(0)
                for i in range(ST):
                    if i + 1 == ST // 2:
                        pool.wait_ge(s_tab, 2 * l + 2)
                    if i + 1 < ST:
                        turn_in(i + 1)
                    turn_out(i)
                wait_apart(pool, s_pv, 6 * l + 6)
                pool.dma_start(gain, at(norm2_g, l)[0:1, :].broadcast_to([P, D])).then_inc(s_gain[1], 16)
                rsqrt_rows(2 * l + 1)


        @block.scalar
        def _(act):
            def slots(S, n):
                act.wait_ge(S.gath, n + 1)
                act.copy(xTe, PS[:, 0:2, :].rearrange("p b n -> p (b n)")).then_inc(S.xte, 1)
                wait_product(act, S.gate, n)
                act.activation(es, PS[:, 2, :], ACT.Exp, scale=-1.0).then_inc(S.eg, 1)
                act.wait_ge(S.hps, n + 1)
                act.copy(hTe, PS[:, 4, :]).then_inc(S.hte, 1)
                wait_product(act, S.down, n)
                act.copy(Y, PS[:, 6:8, :].rearrange("p b n -> p (b n)")).then_inc(S.ys, 1)

            def half_turned(n, j):
                for b in (1, 3):
                    act.wait_ge(s_xT, 8 * n + 4 * j + b + 1)
                    act.copy(hT[:, 2 * b:2 * b + 2, :].rearrange("p k t -> p (k t)"), PS[:, b, :]).then_inc(s_hTa, 1)

            act.dma_start(cst[:, :], consts).then_inc(s_cst, 16)
            act.dma_start(xres[:, :, :], x_v).then_inc(s_x, 16)
            act.wait_ge(s_cst, 16)
            with act.Fori(0, L) as l:
                half_turned(l, 0)
                act.wait_ge(s_pc, l + 1)
                act.activation(dtc, pc[:, R_DT:R_DT + ST], ACT.Exp).then_inc(s_dt, 1)
                act.wait_ge(s_lr, l + 1)
                act.activation(mag, t0, ACT.Exp).then_inc(s_mag, 1)
                act.wait_ge(s_pj, 12 * l + 1)
                act.copy(uT[:, :, :].rearrange("p a n -> p (a n)"), PS[:, 0, :]).then_inc(s_uT, 1)
                act.wait_ge(s_cvz, l + 1)
                for c in range(2):
                    act.wait_ge(s_pj, 12 * l + (3 + c))
                    act.copy(conv[:, 2 * c:2 * c + 2, 3:T + 3],
                             PS[:, 2 + c, :].rearrange("p (a t) -> p a t", a=2)).then_inc(s_cv, 1)
                act.wait_ge(s_cTp, l + 1)
                act.copy(cT[:, :, :].rearrange("p a n -> p (a n)"), PS[:, 5, :]).then_inc(s_cT, 1)
                act.wait_ge(s_gf, l + 1)
                act.activation(gr[:, 2, :], gr[:, 1, :], ACT.Exp)
                act.drain()
                act.activation(gr[:, 2, :], gr[:, 2, :], ACT.Ln, bias=1.0).then_inc(s_gl, 1)
                for j in range(NT):
                    act.wait_ge(s_pj, 12 * l + (5 + j))
                    act.copy(vm[:, j, :], PS[:, j, 0:256]).then_inc(s_vm, 1)
                    act.activation(so[:, j, :], PS[:, j, 256:512], ACT.Exp, scale=-1.0).then_inc(s_oe, 1)
                act.wait_ge(s_cy, l + 1)
                act.activation(scr[:, :], qkm[:, :, :].rearrange("p c t -> p (c t)"), ACT.Exp,
                               scale=-1.0).then_inc(s_ce, 1)
                for a in range(2):
                    for j in range(NT):
                        act.wait_ge(s_pj, 12 * l + (7 + 2 * a + j))
                        act.copy(qk[:, j, a, :], PS[:, 2 * (1 - a) + j, :]).then_inc(s_aq, 1)
                    if a == 0:
                        for hf, ready in enumerate((s_fracv, s_frac)):
                            r = slice(4 * hf, 4 * hf + 4)
                            act.wait_ge(ready, l + 1)
                            act.activation(tab[:, 0, r, :], tab[:, 0, r, :], ACT.Sin, scale=TURN)
                            act.activation(tab[:, 1, r, :], tab[:, 1, r, :], ACT.Sin, scale=TURN).then_inc(s_tab, 1)

                def rms(out_, in_, w):
                    act.activation(out_, in_, ACT.Ln, bias=eps, scale=1.0 / w)
                    act.drain()
                    return act.activation(out_, out_, ACT.Exp, scale=-0.5)

                def copy_bu(i):
                    act.wait_ge(s_bup, ST * l + (i + 1))
                    if i >= 2:
                        act.wait_ge(s_y, ST * l + (i - 1))
                    act.copy(bu[:, i % 2, :, :].rearrange("p c t -> p (c t)"), PS[:, 6, :]).then_inc(s_bu, 1)

                act.wait_ge(s_gT, l + 1)
                act.activation(emt, aT[:, :, 1, :], ACT.Exp).then_inc(s_fl, 1)
                act.wait_ge(s_bTp, l + 1)
                act.copy(bT[:, :, :].rearrange("p a n -> p (a n)"), PS[:, 6, :]).then_inc(s_bT, 1)
                copy_bu(0)
                for h in range(MH):
                    act.wait_ge(s_dp, MH * l + (h + 1))
                    if h >= 2:
                        act.wait_ge(s_pm, MH * l + (h - 1))
                    act.activation(dec[:, h % 2, 0:256], PS[:, 4, 0:256], ACT.Exp, bias=aT[:, 0, 0, h:h + 1])
                    act.activation(dec[:, h % 2, 256:384], PS[:, 4, 256:384], ACT.Exp,
                                   bias=aT[:, 1, 0, h:h + 1]).then_inc(s_de, 1)
                    if h == 0:
                        act.wait_ge(s_qn, l + 1)
                        rms(qss, qss, HD).then_inc(s_qr, 1)
                    copy_bu(1 + h)
                for j in range(NT):
                    act.wait_ge(s_pj, 12 * l + (11 + j))
                    act.copy(av[:, j, :], PS[:, 2 + j, :]).then_inc(s_av, 1)
                act.wait_ge(s_msq, l + 1)
                rms(mss, mss, HD).then_inc(s_mrs, 1)
                copy_bu(5)
                for u in range(6):
                    j, w, hs = unit(u)
                    act.wait_ge(s_mx, 6 * l + (u + 1))
                    if u >= 2:
                        act.wait_ge(s_pTp, 6 * l + (u - 1))
                    for i, h in enumerate(hs):
                        last = act.activation(prob[:, u % 2, w * i:w * i + w], PS[:, u % 2, w * i:w * i + w], ACT.Exp,
                                              bias=amx[:, j, h:h + 1], scale=0.125,
                                              accum_out=ars[:, j, h:h + 1])
                    last.then_inc(s_pr, 1)
                    if u in (1, 3):
                        copy_bu(5 + (u + 1) // 2)
                act.wait_ge(s_ge, l + 1)
                act.activation(scr[:, 512:1024], scr[:, 512:1024], ACT.Exp, scale=-1.5957691216057308).then_inc(s_gx, 1)
                for j in range(NT):
                    act.wait_ge(s_osq, 2 * l + (j + 1))
                    rms(oss[:, j, :], oss[:, j, :], HD).then_inc(s_ors, 1)
                act.wait_ge(s_glu, l + 1)
                for c in range(2):
                    last = act.activation(scr[:, 512 + T * c:512 + T * c + T], PS[:, 6, T * c:T * c + T], ACT.Exp,
                                          bias=ngb[:, c:c + 1], scale=-1.0)
                last.then_inc(s_glx, 1)
                act.wait_ge(s_ym, l + 1)
                act.activation(scr[:, 512:1024], PS[:, 7, :], ACT.Ln, bias=eps)
                act.drain()
                act.activation(scr[:, 512:1024], scr[:, 512:1024], ACT.Exp, scale=-0.5).then_inc(s_yr, 1)
                half_turned(l, 1)
                act.wait_ge(s_rg, l + 1)
                act.activation(pex, pex, ACT.Exp).then_inc(s_rge, 1)
                act.wait_ge(s_rv, l + 1)
                act.activation(dif, dif, ACT.Exp).then_inc(s_rve, 1)
                with act.Fori(0, NG) as g:
                    slots(G, l * NG + g)
                wait_apart(act, s_ctl, l + 1)
                n_u = act.value_load(ctl[0:1, 0:1], min_val=1, max_val=MAXU - 1)
                u_0 = act.value_load(ctl[0:1, 1:2], min_val=0, max_val=L * (MAXU - 1))
                with act.Fori(0, n_u) as u:
                    slots(U, u_0 + u)

        @block.vector
        def _(dve):
            V = nc.vector
            V.memset(conv[:, :, 0:3], 0.0).then_inc(s_cvz, 1)
            V.memset(before[:, :], 0.0).then_inc(s_xf, 1)
            V.drain()

            def norm_rows(n, l, gi):
                for j in range(NT):
                    V.tensor_tensor_reduce(xs[:, j, :], xres[:, j, :], xres[:, j, :], 1.0, 0.0, ALU.mult, ALU.add,
                                           ss[:, j:j + 1])
                V.drain()
                V.tensor_scalar(ss, ss, 1.0 / D, EPS, ALU.mult, ALU.add).then_inc(s_ss, 1)
                dve.wait_ge(s_rs, 2 * l + (gi + 1))
                dve.wait_ge(s_gain[gi], 16 * l + 16)
                for j in range(NT):
                    last = V.scalar_tensor_tensor(xs[:, j, :], xres[:, j, :], rs[:, j:j + 1], gain, ALU.mult, ALU.mult)
                last.then_inc(s_xs, 1)
                for b in (0, 2):
                    dve.wait_ge(s_xT, 8 * l + (4 * gi + b + 1))
                    V.tensor_copy(hT[:, 2 * b:2 * b + 2, :].rearrange("p k t -> p (k t)"), PS[:, b, :]).then_inc(s_hTv, 1)

            def slots(S, n, s):
                iota = cst[:, C_T:C_T + P]
                for j in range(NT):
                    V.tensor_scalar(hit[:, 0, j, :], iota, s[:, j, 0:1], None, ALU.is_equal)
                    V.tensor_scalar(hitw[:, j, :], iota, s[:, j, 0:1], wgt[:, j, 0:1], ALU.is_equal, ALU.mult)
                    V.tensor_scalar(hit2[:, j, :], iota, s[:, j, 1:2], wgt[:, j, 1:2], ALU.is_equal, ALU.mult)
                V.drain()
                for j in range(NT):
                    V.tensor_tensor(hitw[:, j, :], hitw[:, j, :], hit2[:, j, :], ALU.add)
                    last = V.scalar_tensor_tensor(hit[:, 0, j, :], iota, s[:, j, 1:2], hit[:, 0, j, :], ALU.is_equal,
                                                  ALU.add)
                last.then_inc(S.hit, 1)
                V.drain()
                V.tensor_scalar(s, s, -float(P), None, ALU.add)
                dve.wait_ge(S.wt, n + 1)
                V.tensor_copy(hitT.rearrange("p j t -> p (j t)"), PS[:, 5, 0:256]).then_inc(S.wpt, 1)
                dve.wait_ge(S.eg, n + 1)
                V.tensor_scalar(es, es, 1.0, None, ALU.add)
                V.drain()
                V.reciprocal(es, es)
                V.drain()
                V.tensor_tensor(es, es, PS[:, 2, :], ALU.mult)
                V.drain()
                wait_product(dve, S.up, n)
                V.tensor_tensor(hx, es, PS[:, 3, :], ALU.mult).then_inc(S.h, 1)
                dve.wait_ge(S.comb, n + 1)
                for j in range(NT):
                    V.tensor_tensor(xres[:, j, :], xres[:, j, :], PS[:, 2 * j:2 * j + 2, :].rearrange("p b n -> p (b n)"),
                                    ALU.add)
                V.drain()

            def bcast(ap, n):
                return ap.unsqueeze(len(ap.shape)).broadcast_to(list(ap.shape) + [n])

            dve.wait_ge(s_cst, 16)
            dve.wait_ge(s_x, 16)
            with dve.Fori(0, L) as l:
                dve.wait_ge(s_par, l * (16 * NPAR) + 16 * NPAR)
                V.tensor_copy(ldt[:, 2:2 + P].rearrange("i (a s) -> i a s", a=2),
                              ldt[:, 0:2].unsqueeze(2).broadcast_to([ST, 2, SS])).then_inc(s_dr, 1)
                norm_rows(2 * l, l, 0)

                dve.wait_ge(s_pcp, l + 1)
                V.tensor_copy(pc[:, :], PS[:, 4, 0:NR]).then_inc(s_pc, 1)
                V.drain()
                cm = scr[:, 0:512].rearrange("p (r c a s) -> p r c a s", r=2, c=2, a=2)
                msk = cst[:, C_CMASK:C_CMASK + P].rearrange("p (a s) -> p a s", a=2)
                for r, sign in enumerate((1.0, -1.0)):
                    for c in range(2):
                        last = V.scalar_tensor_tensor(cm[:, r, c], msk, sign,
                                                      cmat[:, r, c, :].unsqueeze(1).broadcast_to([P, 2, SS]),
                                                      ALU.mult, ALU.mult)
                last.then_inc(s_cm, 1)
                V.tensor_scalar(ngb, pc[:, R_GB:R_GB + 2], -1.0, None, ALU.mult)

                lr, li = pc[:, R_LR:R_LR + ST], pc[:, R_LI:R_LI + ST]
                dve.wait_ge(s_dt, l + 1)
                V.tensor_tensor(t0, lr, dtc, ALU.mult).then_inc(s_lr, 1)
                V.tensor_tensor(t1, li, dtc, ALU.mult)
                V.drain()
                V.tensor_scalar(t1, t1, 0.15915494309189535, None, ALU.mult)
                V.drain()
                V.tensor_scalar(phih, t1, ROUND, -ROUND, ALU.add, ALU.add)
                V.drain()
                V.tensor_tensor(t1, t1, phih, ALU.subtract)
                V.drain()
                V.tensor_scalar(phih, t1, GRID, -GRID, ALU.add, ALU.add)
                V.drain()
                V.tensor_tensor(phil, t1, phih, ALU.subtract).then_inc(s_phi, 1)

                dve.wait_ge(s_pj, 12 * l + 2)
                gf, gn, gl, gB, ga, gM = (gr[:, i, :] for i in range(6))
                V.tensor_scalar(gf, PS[0:MH, 1, 256:512], bi[:, 1:2], None, ALU.add)
                V.tensor_scalar(ga, PS[0:MH, 1, 0:256], bi[:, 0:1], None, ALU.add)
                V.drain()
                V.scalar_tensor_tensor(gn, gf, -1.0, gf, ALU.mult, ALU.min).then_inc(s_gf, 1)

                phases(V, 0, qkm[:, :, :]).then_inc(s_fracv, 1)
                V.drain()

                for c in range(4):
                    if c % 2 == 0:
                        dve.wait_ge(s_cv, 2 * l + (c // 2 + 1))
                    V.tensor_scalar(qkm[:, c, :], conv[:, c, 0:T], pc[:, R_CW + c:R_CW + c + 1],
                                    pc[:, R_CB + c:R_CB + c + 1], ALU.mult, ALU.add)
                for k in range(1, 4):
                    V.drain()
                    if k == 3:
                        dve.wait_ge(s_cTp, l + 1)
                    for c in range(4):
                        last = V.scalar_tensor_tensor(qkm[:, c, :], conv[:, c, k:k + T],
                                                      pc[:, R_CW + 4 * k + c:R_CW + 4 * k + c + 1], qkm[:, c, :],
                                                      ALU.mult, ALU.add)
                last.then_inc(s_cy, 1)

                dve.wait_ge(s_gl, l + 1)
                V.scalar_tensor_tensor(gf, gf, 0.0, gl, ALU.min, ALU.subtract)
                V.drain()
                V.tensor_tensor_scan(gB, cst[0:MH, C_ONES:C_ONES + 1].broadcast_to([MH, T]), gf, 0.0, ALU.mult, ALU.add)
                V.drain()
                V.tensor_tensor(ga, ga, gB, ALU.subtract)
                V.drain()
                V.tensor_tensor_scan(gM, ga, ga, 0.0, ALU.max, ALU.max)
                V.drain()
                V.scalar_tensor_tensor(gB, gB, -1.0, gM, ALU.mult, ALU.subtract)
                V.tensor_scalar(gM, gM, -1.0, None, ALU.mult).then_inc(s_gm, 1)

                dve.wait_ge(s_ce, l + 1)
                qf = qkm[:, :, :].rearrange("p c t -> p (c t)")
                V.tensor_scalar(scr[:, :], scr[:, :], 1.0, None, ALU.add)
                V.drain()
                V.reciprocal(scr[:, :], scr[:, :])
                V.drain()
                V.tensor_tensor(qf, qf, scr[:, :], ALU.mult).then_inc(s_qkm, 1)
                dve.wait_ge(s_oe, 2 * l + 2)
                sf = so[:, :, :].rearrange("p j n -> p (j n)")
                V.tensor_scalar(sf, sf, 1.0, None, ALU.add)
                V.drain()
                V.reciprocal(sf, sf)

                dve.wait_ge(s_gTp, l + 1)
                V.tensor_copy(aT.rearrange("p j w h -> p (j w h)"), PS[:, 4, 0:16]).then_inc(s_gT, 1)
                va, vb = scr[:, 0:256], scr[:, 256:512]

                def turn_in(i):
                    b = i % 2
                    dve.wait_ge(s_bu, ST * l + (i + 1))
                    if i >= 2:
                        dve.wait_ge(s_xi, ST * l + (i - 1))
                    V.tensor_tensor(va, tab[:, 0, i, :], bu[:, b, 0, :], ALU.mult)
                    V.tensor_tensor(vb, tab[:, 1, i, :], bu[:, b, 1, :], ALU.mult)
                    V.drain()
                    V.tensor_tensor(zz[:, b, 0, :], va, vb, ALU.add)
                    V.drain()
                    V.tensor_tensor_scan(zz[:, b, 0, :], mag[:, i:i + 1].broadcast_to([P, T]), zz[:, b, 0, :], 0.0,
                                         ALU.mult, ALU.add)

                def turn_out(i):
                    b = i % 2
                    dve.wait_ge(s_wi, ST * l + (i + 1))
                    V.tensor_tensor_scan(zz[:, b, 1, :], mag[:, i:i + 1].broadcast_to([P, T]), zz[:, b, 1, :], 0.0,
                                         ALU.mult, ALU.add).then_inc(s_zi, 1)
                    V.drain()
                    V.tensor_tensor(va, tab[:, 0, i, :], zz[:, b, 0, :], ALU.mult)
                    V.tensor_tensor(vb, tab[:, 1, i, :], zz[:, b, 1, :], ALU.mult)
                    V.drain()
                    V.tensor_tensor(bu[:, b, 0, :], va, vb, ALU.subtract).then_inc(s_xr, 1)
                    V.drain()

                def discrete_b():
                    dve.wait_ge(s_tab, 2 * l + 2)
                    dve.wait_ge(s_mag, l + 1)
                    are, aim = scr[:, 0:8], scr[:, 8:16]
                    V.tensor_tensor(are, mag, tab[:, 0, :, 1], ALU.mult)
                    V.tensor_tensor(aim, mag, tab[:, 1, :, 1], ALU.mult)
                    V.tensor_tensor(den, lr, lr, ALU.mult)
                    V.tensor_tensor(t1, li, li, ALU.mult)
                    V.drain()
                    V.tensor_scalar(are, are, -1.0, None, ALU.add)
                    V.tensor_tensor(den, den, t1, ALU.add)
                    V.drain()
                    V.reciprocal(den, den)
                    V.tensor_tensor(fr, are, lr, ALU.mult)
                    V.tensor_tensor(fi, aim, lr, ALU.mult)
                    V.tensor_tensor(t0, aim, li, ALU.mult)
                    V.tensor_tensor(t1, are, li, ALU.mult)
                    V.drain()
                    V.tensor_tensor(fr, fr, t0, ALU.add)
                    V.tensor_tensor(fi, fi, t1, ALU.subtract)
                    V.drain()
                    V.tensor_tensor(fr, fr, den, ALU.mult)
                    V.tensor_tensor(fi, fi, den, ALU.mult)
                    V.drain()
                    bb = scr[:, 512:1024].rearrange("p (r i a h) -> p r i a h", r=2, i=ST, a=2)
                    pp = scr[:, 0:512].rearrange("p (n i h) -> p n i h", n=4, i=ST)
                    V.memset(scr[:, 512:1024], 0.0)
                    V.tensor_tensor(pp[:, 0], bmat[:, 0], bcast(fr, SH), ALU.mult)
                    V.tensor_tensor(pp[:, 1], bmat[:, 1], bcast(fi, SH), ALU.mult)
                    V.tensor_tensor(pp[:, 2], bmat[:, 1], bcast(fr, SH), ALU.mult)
                    V.tensor_tensor(pp[:, 3], bmat[:, 0], bcast(fi, SH), ALU.mult)
                    V.drain()
                    for a in range(2):
                        r = slice(64 * a, 64 * a + 64)
                        V.tensor_tensor(bb[r, 0, :, a, :], pp[r, 0], pp[r, 1], ALU.subtract)
                        last = V.tensor_tensor(bb[r, 1, :, a, :], pp[r, 2], pp[r, 3], ALU.add)
                    last.then_inc(s_bb, 1)

                discrete_b()
                V.drain()

                for a in range(2):
                    for j in range(NT):
                        dve.wait_ge(s_aq, 4 * l + (2 * a + j + 1))
                        V.tensor_tensor(scr[:, 0:512], qk[:, j, a, :], qk[:, j, a, :], ALU.mult)
                        V.drain()
                        last = V.tensor_reduce(qss[:, j, a, :], scr[:, 0:512].rearrange("p (h d) -> p h d", h=AH), X,
                                               ALU.add)
                        V.drain()
                last.then_inc(s_qn, 1)
                turn_in(0)

                def rotated(n):
                    a, j = n // 2, n % 2
                    if n == 0:
                        dve.wait_ge(s_qr, l + 1)
                    v = qk[:, j, a, :].rearrange("p (h d) -> p h d", h=AH)
                    V.tensor_tensor(v, v, bcast(qss[:, j, a, :], HD), ALU.mult)
                    V.drain()
                    V.tensor_tensor(v, v, qkg[:, a, :].unsqueeze(1).broadcast_to([P, AH, HD]), ALU.mult)
                    V.drain()
                    cs = cst[:, C_COS + 8 * j:C_COS + 8 * j + 8].unsqueeze(1).broadcast_to([P, AH, 8])
                    sn = cst[:, C_SIN + 8 * j:C_SIN + 8 * j + 8].unsqueeze(1).broadcast_to([P, AH, 8])
                    w = scr[:, 0:256].rearrange("p (n h d) -> p n h d", n=4, h=AH)
                    V.tensor_tensor(w[:, 0], v[:, :, 0:8], cs, ALU.mult)
                    V.tensor_tensor(w[:, 1], v[:, :, 8:16], sn, ALU.mult)
                    V.tensor_tensor(w[:, 2], v[:, :, 8:16], cs, ALU.mult)
                    V.tensor_tensor(w[:, 3], v[:, :, 0:8], sn, ALU.mult)
                    V.drain()
                    V.tensor_tensor(v[:, :, 0:8], w[:, 0], w[:, 1], ALU.subtract)
                    V.tensor_tensor(v[:, :, 8:16], w[:, 2], w[:, 3], ALU.add).then_inc(s_qkn, 1)
                    V.drain()

                for h in range(MH):
                    dve.wait_ge(s_de, MH * l + (h + 1))
                    dve.wait_ge(s_sp, MH * l + (h + 1))
                    if h >= 1:
                        dve.wait_ge(s_np, MH * l + h)
                    else:
                        dve.wait_ge(s_frac, l + 1)
                    V.scalar_tensor_tensor(pm, PS[:, 5, 0:384], 0.125, dec[:, h % 2, :], ALU.mult,
                                           ALU.mult).then_inc(s_pm, 1)
                    rotated(h)
                    if h + 1 < MH:
                        if h == 0:
                            turn_in(1)
                        turn_out(h)
                        if h > 0:
                            turn_in(h + 1)
                dve.wait_ge(s_np, MH * l + MH)
                V.memset(conv[:, :, 0:3], 0.0).then_inc(s_cvz, 1)
                dve.wait_ge(s_fl, l + 1)
                V.tensor_copy(mden, PS[:, 5, 384:392].rearrange("p (j h) -> p j h", j=NT))
                V.drain()
                V.scalar_tensor_tensor(mden, mden, -1.0, mden, ALU.mult, ALU.max)
                V.drain()
                V.tensor_tensor(mden, mden, emt, ALU.max)
                V.drain()
                V.reciprocal(mden, mden)
                V.drain()
                hm = qkm[:, 0:2, :].rearrange("p c (h d) -> p c h d", h=MH)
                V.tensor_tensor(hm, PS[:, 0, :].rearrange("p (j h d) -> p j h d", j=NT, h=MH), bcast(mden, HD), ALU.mult)
                V.drain()
                V.tensor_tensor(scr[:, 0:512].rearrange("p (j h d) -> p j h d", j=NT, h=MH), hm, hm, ALU.mult)
                V.drain()
                V.tensor_reduce(mss, scr[:, 0:512].rearrange("p (j h d) -> p j h d", j=NT, h=MH), X,
                                ALU.add).then_inc(s_msq, 1)

                turn_out(3)
                for n in range(4):
                    a, j = n // 2, n % 2
                    dve.wait_ge(s_qTp, 4 * l + (n + 1))
                    V.tensor_copy(qkT[:, a, :, P * j:P * j + P],
                                  PS[:, QK_BANK[n], :].rearrange("p (c t) -> p c t", c=4)).then_inc(s_qT, 1)
                turn_in(4)

                dve.wait_ge(s_mrs, l + 1)
                V.tensor_tensor(hm, hm, bcast(mss, HD), ALU.mult)
                V.drain()
                hf_ = qkm[:, 0:2, :].rearrange("p c n -> p (c n)")
                V.tensor_tensor(hf_, hf_, sf, ALU.mult).then_inc(s_hm, 1)

                def mix_m():
                    dve.wait_ge(s_hmT, l + 1)
                    for c in range(2):
                        last = V.tensor_scalar(mixT[:, c, :], PS[:, 0, T * c:T * c + T], pc[:, R_MG + c:R_MG + c + 1],
                                               None, ALU.mult)
                    last.then_inc(s_mixm, 1)

                def maxima(u):
                    j, w, hs = unit(u)
                    m = amx[:, j, hs.start:hs.stop:2]
                    dve.wait_ge(s_as, 6 * l + (u + 1))
                    V.tensor_reduce(m, PS[:, u % 2, :].rearrange("p (h k) -> p h k", k=w), X, ALU.max)
                    V.drain()
                    V.tensor_scalar(m, m, -0.125, None, ALU.mult).then_inc(s_mx, 1)

                def turned(u):
                    dve.wait_ge(s_pTp, 6 * l + (u + 1))
                    if u >= 2:
                        dve.wait_ge(s_pv, 6 * l + (u - 1))
                    V.tensor_copy(probT[:, u % 2, :], PS[:, 2 + u % 2, :]).then_inc(s_pT, 1)

                def heads(j):
                    dve.wait_ge(s_pv, 6 * l + (2 if j == 0 else 6))
                    dve.wait_ge(s_pr, 6 * l + (2 if j == 0 else 6))
                    V.reciprocal(ars[:, j, :], ars[:, j, :])
                    V.drain()
                    o = qk[:, j, 0, :].rearrange("p (h d) -> p h d", h=AH)
                    V.tensor_tensor(o, PS[:, 4 + j, :].rearrange("p (h d) -> p h d", h=AH), bcast(ars[:, j, :], HD), ALU.mult)
                    V.drain()
                    V.tensor_tensor(sf, qk[:, j, 0, :], qk[:, j, 0, :], ALU.mult)
                    V.drain()
                    V.tensor_reduce(oss[:, j, :], sf.rearrange("p (h d) -> p h d", h=AH), X,
                                    ALU.add).then_inc(s_osq, 1)
                    dve.wait_ge(s_ors, 2 * l + (j + 1))
                    V.tensor_tensor(o, o, bcast(oss[:, j, :], HD), ALU.mult).then_inc(s_on, 1)

                mix_m()
                turn_out(4)
                maxima(0)
                maxima(1)
                turn_in(5)
                turned(0)
                turned(1)
                turn_out(5)
                maxima(2)
                maxima(3)
                turn_in(6)
                turned(2)
                turn_out(6)
                maxima(4)
                turned(3)
                turn_in(7)
                maxima(5)
                turn_out(7)
                dve.wait_ge(s_y, ST * l + ST)
                dve.wait_ge(s_xi, ST * l + ST)
                y_, e_ = scr[:, 0:512], scr[:, 512:1024]
                for c in range(2):
                    V.scalar_tensor_tensor(y_[:, T * c:T * c + T], uT[:, c, :], pc[:, R_SD + c:R_SD + c + 1],
                                           PS[:, 7, T * c:T * c + T], ALU.mult, ALU.add)
                V.drain()
                V.tensor_tensor(e_, y_, y_, ALU.mult)
                V.drain()
                V.tensor_scalar(e_, e_, 0.044715, 1.0, ALU.mult, ALU.add)
                V.drain()
                V.tensor_tensor(e_, e_, y_, ALU.mult).then_inc(s_ge, 1)
                turned(4)
                turned(5)
                dve.wait_ge(s_gx, l + 1)
                V.tensor_scalar(e_, e_, 1.0, None, ALU.add)
                V.drain()
                V.reciprocal(e_, e_)
                V.drain()
                V.tensor_tensor(y_, y_, e_, ALU.mult).then_inc(s_z, 1)
                heads(0)
                heads(1)
                for c in range(2):
                    dve.wait_ge(s_onT, 2 * l + (c + 1))
                    for i in range(2):
                        last = V.tensor_scalar(mixT[:, 2 + 2 * c + i, :], PS[:, 2 + c, T * i:T * i + T],
                                               pc[:, R_AG + 2 * c + i:R_AG + 2 * c + i + 1], None, ALU.mult)
                    last.then_inc(s_mixa, 1)

                dve.wait_ge(s_glx, l + 1)
                V.tensor_scalar(e_, e_, 1.0, None, ALU.add)
                V.drain()
                V.reciprocal(e_, e_)
                V.drain()
                V.tensor_tensor(y_, y_, e_, ALU.mult)
                V.drain()
                V.tensor_tensor(e_, y_, y_, ALU.mult).then_inc(s_ysq, 1)
                dve.wait_ge(s_yr, l + 1)
                for c in range(2):
                    last = V.scalar_tensor_tensor(mixT[:, 6 + c, :], y_[:, T * c:T * c + T],
                                                  pc[:, R_SG + c:R_SG + c + 1], e_[:, T * c:T * c + T], ALU.mult, ALU.mult)
                last.then_inc(s_mixs, 1)

                for j in range(NT):
                    dve.wait_ge(s_op, 2 * l + (j + 1))
                    V.tensor_tensor(xres[:, j, :], xres[:, j, :],
                                    PS[:, 2 * j:2 * j + 2, :].rearrange("p b n -> p (b n)"), ALU.add)
                V.drain()
                norm_rows(2 * l + 1, l, 1)

                dve.wait_ge(s_rp, l + 1)
                V.tensor_tensor(lg, PS[:, 0, 0:128].rearrange("p (j n) -> p j n", j=NT)[:, :, 0:36],
                                rb[:, :].unsqueeze(1).broadcast_to([P, NT, 36]), ALU.add)
                V.memset(gl8, -3.0e38)
                V.drain()
                V.tensor_copy(gl8[:, :, 0:4], lg[:, :, 0:4])
                V.drain()
                for j in range(NT):
                    V.max(gmx[:, j, :], gl8[:, j, :])
                V.drain()
                for j in range(NT):
                    V.max_index(idx[:, 0, j, :], gmx[:, j, :], gl8[:, j, :])
                V.tensor_tensor(pex, lg[:, :, 0:4], gmx[:, :, 0:1].broadcast_to([P, NT, 4]), ALU.subtract).then_inc(s_rg, 1)
                V.drain()
                V.tensor_copy(gsel, idx[:, 0, :, 0:1])
                V.drain()
                gid = cst[:, C_GID:C_GID + NE].unsqueeze(1).broadcast_to([P, NT, NE])
                V.tensor_tensor(elp, gid, gsel.broadcast_to([P, NT, NE]), ALU.not_equal)
                V.drain()
                V.scalar_tensor_tensor(elp, elp, NEG, lg[:, :, 4:36], ALU.mult, ALU.add)
                V.drain()
                for j in range(NT):
                    V.max(emx[:, j, :], elp[:, j, :])
                V.drain()
                for j in range(NT):
                    V.max_index(idx[:, 1, j, :], emx[:, j, :], elp[:, j, :])
                V.tensor_tensor(dif, emx[:, :, 1:2], emx[:, :, 0:1], ALU.subtract).then_inc(s_rv, 1)
                V.drain()
                V.tensor_copy(eid, idx[:, 1, :, 0:2])
                dve.wait_ge(s_rge, l + 1)
                V.tensor_reduce(pgs, pex, X, ALU.add)
                V.drain()
                V.reciprocal(pgs, pgs)
                iota_e = cst[:, C_T:C_T + NE].unsqueeze(1).broadcast_to([P, NT, NE])
                for a in range(2):
                    V.tensor_tensor(mk[:, a], iota_e, eid[:, :, a:a + 1].broadcast_to([P, NT, NE]), ALU.is_equal)
                V.drain()
                V.tensor_tensor(mks, mk[:, 0], mk[:, 1], ALU.add).then_inc(s_mk, 1)
                dve.wait_ge(s_rve, l + 1)
                V.tensor_scalar(wgt[:, :, 0:1], dif, 1.0, None, ALU.add)
                V.drain()
                V.reciprocal(wgt[:, :, 0:1], wgt[:, :, 0:1])
                V.drain()
                V.tensor_tensor(wgt[:, :, 0:1], wgt[:, :, 0:1], pgs, ALU.mult)
                V.drain()
                V.tensor_tensor(wgt[:, :, 1:2], wgt[:, :, 0:1], dif, ALU.mult)
                dve.wait_ge(s_rk, l + 1)
                V.tensor_copy(rnk, PS[:, 1, 0:64].rearrange("p (j n) -> p j n", j=NT))
                V.tensor_copy(cnt, PS[:, 1, 64:96])
                V.drain()
                V.tensor_scalar(nu, cnt, float(CAP), None, ALU.is_gt)
                V.drain()
                V.scalar_tensor_tensor(nu, cnt, float(CAP + P), nu, ALU.is_gt, ALU.add)
                V.drain()
                V.tensor_tensor_scan(uend, cst[:, C_ONES:C_ONES + NE], nu, 0.0, ALU.mult, ALU.add)
                V.drain()
                V.tensor_tensor(ust, uend, nu, ALU.subtract)
                V.tensor_scalar(cmp_, uend, cst[:, C_P:C_P + 1], None, ALU.is_le)
                V.drain()
                V.tensor_reduce(euc, cmp_, X, ALU.add)
                V.drain()
                V.tensor_scalar(euc, euc, float(NE - 1), None, ALU.min).then_inc(s_eu, 1)
                for a in range(2):
                    V.tensor_tensor(rtm, mk[:, a], rnk, ALU.mult)
                    V.drain()
                    V.tensor_reduce(rkk[:, :, a:a + 1], rtm, X, ALU.add)
                    V.drain()
                    V.tensor_tensor(rtm, mk[:, a], ust.unsqueeze(1).broadcast_to([P, NT, NE]), ALU.mult)
                    V.drain()
                    V.tensor_reduce(usk[:, :, a:a + 1], rtm, X, ALU.add)
                    V.drain()
                V.tensor_scalar(far, rkk, float(CAP), BIG, ALU.is_ge, ALU.mult)
                V.scalar_tensor_tensor(sg, eid, float(CAP), rkk, ALU.mult, ALU.add)
                V.scalar_tensor_tensor(su, usk, float(P), rkk, ALU.mult, ALU.add)
                V.drain()
                V.tensor_tensor(sg, sg, far, ALU.subtract)
                V.tensor_tensor(su, su, far, ALU.add)
                V.drain()
                V.tensor_scalar(su, su, -(float(CAP) + BIG), None, ALU.add)
                V.tensor_scalar(one1, uend[0:1, NE - 1:NE], 1.0, None, ALU.max)
                V.drain()
                V.tensor_copy(ctl[:, 0:1], one1)
                V.tensor_copy(ctl[:, 1:2], before[:, 0:1])
                V.drain()
                V.tensor_tensor(before[:, 0:1], before[:, 0:1], one1, ALU.add)
                dve.wait_ge(s_eup, l + 1)
                V.tensor_copy(ctl[:, 2:2 + MAXU], PS[0:1, 1, 128:128 + MAXU]).then_inc(s_ctl, 1)
                with dve.Fori(0, NG) as g:
                    slots(G, l * NG + g, sg)
                wait_apart(dve, s_ctl, l + 1)
                n_u = dve.value_load(ctl[0:1, 0:1], min_val=1, max_val=MAXU - 1)
                u_0 = dve.value_load(ctl[0:1, 1:2], min_val=0, max_val=L * (MAXU - 1))
                with dve.Fori(0, n_u) as u:
                    slots(U, u_0 + u, su)
                V.tensor_copy(before[:, 1:2], one1).then_inc(s_xf, 1)

        @block.tensor
        def _(pe):
            def turn_xs(l, gi):
                pe.wait_ge(s_xs, 2 * l + (gi + 1))
                for k in range(KD):
                    for j in range(NT):
                        o = (k % 2) * T + j * P
                        last = pe.transpose(PS[:, k // 2, o:o + P], xs[:, j, k::KD], ident)
                    if k % 2:
                        last.then_inc(s_xT, 1)
                pe.wait_ge(s_hTv, 4 * l + (2 * gi + 2))
                pe.wait_ge(s_hTa, 4 * l + (2 * gi + 2))

            def slots(S, n, strips):
                pe.wait_ge(S.hit, n + 1)
                for k in range(KD):
                    for j in range(NT):
                        last = pe.matmul(PS[:, k // 4, P * (k % 4):P * (k % 4) + P], xs[:, j, k::KD], hit[:, 0, j, :],
                                         start=j == 0, stop=j == NT - 1)
                last.then_inc(S.gath, 1)
                for j in range(NT):
                    last = pe.transpose(PS[:, 5, P * j:P * j + P], hitw[:, j, :], ident)
                last.then_inc(S.wt, 1)
                pe.wait_ge(S.xte, n + 1)
                m = P // strips
                for kind, bank in ((0, 2), (1, 3)):
                    for k in range(KD):
                        arrived(n, kind, k, KD)
                        for j in range(strips):
                            last = pe.matmul(PS[m * j:m * j + m, bank, :], xTe[:, P * k + m * j:P * k + m * j + m],
                                             weight(kind, j, k, 0), start=k == 0, stop=k == KD - 1)
                        used(last, kind, k, KD)
                pe.wait_ge(S.h, n + 1)
                for c in range(KF):
                    last = pe.transpose(PS[:, 4, P * c:P * c + P], hx[:, c::KF], ident)
                last.then_inc(S.hps, 1)
                pe.wait_ge(S.hte, n + 1)
                for c in range(KF):
                    arrived(n, 2, c, KF)
                    for n2 in range(2):
                        for j in range(strips):
                            last = pe.matmul(PS[m * j:m * j + m, 6 + n2, :], hTe[:, P * c + m * j:P * c + m * j + m],
                                             weight(2, j, c, n2), start=c == 0, stop=c == KF - 1)
                    used(last, 2, c, KF)
                pe.wait_ge(S.ys, n + 1)
                pe.wait_ge(S.wpt, n + 1)
                for j in range(NT):
                    for n2 in range(2):
                        last = pe.matmul(PS[:, 2 * j + n2, :], hitT[:, j, :], Y[:, 512 * n2:512 * n2 + 512],
                                         start=True, stop=True)
                last.then_inc(S.comb, 1)

            def quarter(kind, k, n):
                q = 2 * kind + 2 * k // n
                return (q + 1) % 3, q // 3

            def group_arrived(n, kind, k, nk):
                if k % (nk // 2) == 0:
                    r, i = quarter(kind, k, nk)
                    pe.wait_ge(s_q[r], n * 32 + (16 * i + 16))

            def group_weight(kind, j, k, n2):
                nk = KD if kind < 2 else KF
                w = D * DE // P // nk
                o = 2048 * j + w * (k % (nk // 2)) + 512 * n2
                return ring[:, quarter(kind, k, nk)[0], o:o + 512]

            def group_used(last, kind, k, nk):
                if k % (nk // 2) == nk // 2 - 1:
                    last.then_inc(s_sub, 1)

            def unit_arrived(n, kind, k, nk):
                if k == 0:
                    pe.wait_ge(s_ow[kind], n * 16 + 16)

            def unit_weight(kind, j, k, n2):
                o = 4096 * (2 + kind) + (512 * k if kind < 2 else 1024 * k + 512 * n2)
                return flat[:, o:o + 512]

            def unit_used(last, kind, k, nk):
                if k == nk - 1:
                    last.then_inc(s_ou[kind], 1)

            for s in s_ou:
                pe.sem_inc(s, 1)
            pe.wait_ge(s_cst, 16)
            with pe.Fori(0, L) as l:
                wait_apart(pe, s_par, l * (16 * NPAR) + 16 * NPAR)
                pe.transpose(PS[:, 4, 0:R_DT], rows[:, :], ident[0:R_DT, 0:R_DT])
                wait_apart(pe, s_dr, l + 1)
                pe.transpose(PS[:, 4, R_DT:NR], ldt[:, 2:2 + P], ident[0:ST, 0:ST]).then_inc(s_pcp, 1)
                turn_xs(l, 0)

                def by_feature(job, bank, half, c, col, m, o=0):
                    for k in range(KD):
                        last = pe.matmul(PS[o:o + m, bank, T * half:T * half + T], wchunk(c)[:, k, col:col + m],
                                         hT[:, k, :], start=k == 0, stop=k == KD - 1)
                    if job:
                        last.then_inc(s_pj, 1)

                def by_token(j, bank, c):
                    for k in range(KD):
                        last = pe.matmul(PS[:, bank, :], hT[:, k, P * j:P * j + P], wchunk(c)[:, k, 0:512],
                                         start=k == 0, stop=k == KD - 1)
                    last.then_inc(s_pj, 1)

                pe.wait_ge(s_win[0], 32 * l + 32)
                by_feature(0, 0, 0, 0, 0, P)
                by_feature(1, 0, 1, 0, P, P)
                by_feature(0, 1, 0, 0, 256, MH)
                by_feature(1, 1, 1, 0, 260, MH)
                pe.wait_ge(s_win[1], 16 * l + 16)
                for c in range(4):
                    by_feature(c % 2, 2 + c // 2, c % 2, 1, P * c, P)
                pe.wait_ge(s_cm, l + 1)
                for i in range(4):
                    last = pe.transpose(PS[:, 5, P * i:P * i + P], scr[:, P * i:P * i + P], ident)
                last.then_inc(s_cTp, 1)
                pe.wait_ge(s_win[2], 16 * l + 16)
                pe.wait_ge(s_uT, l + 1)
                by_token(0, 0, 2)
                pe.wait_ge(s_gf, l + 1)
                by_token(1, 1, 2)
                pe.wait_ge(s_win[3], 16 * l + 16)
                for j in range(NT):
                    pe.wait_ge(s_cv, 2 * l + (j + 1))
                    by_token(j, 2 + j, 3)
                wait_apart(pe, s_gm, l + 1)
                for j in range(NT):
                    for w, r in enumerate((4, 3)):
                        o = 8 * j + 4 * w
                        last = pe.transpose(PS[:, 4, o:o + MH], gr[:, r, P * j:P * j + P], ident[0:MH, 0:MH])
                last.then_inc(s_gTp, 1)
                pe.wait_ge(s_win[4], 16 * l + 16)
                for j in range(NT):
                    pe.wait_ge(s_oe, 2 * l + (j + 1))
                    by_token(j, j, 4)

                mqk = cst[:, C_MQK:C_MQK + P]

                def decay(h):
                    if h == 0:
                        pe.wait_ge(s_gT, l + 1)
                    else:
                        pe.wait_ge(s_de, MH * l + h)
                    for o, t0_, n in ((0, 0, T), (T, P, P)):
                        pe.matmul(PS[:, 4, o:o + n], cst[0:MH, C_SEL + P * h:C_SEL + P * h + P],
                                  gr[:, 5, t0_:t0_ + n], start=True, stop=False)
                        last = pe.matmul(PS[:, 4, o:o + P], mqk, ident, start=False, stop=True)
                    last.then_inc(s_dp, 1)

                def score(h):
                    r = slice(64 * (h % 2), 64 * (h % 2) + 64)
                    for o, s0, t0_, n in ((0, 0, 0, T), (T, P, P, P)):
                        last = pe.matmul(PS[:, 5, o:o + n], qkm[r, 2 + h // 2, s0:s0 + P], qkm[r, h // 2, t0_:t0_ + n],
                                         start=True, stop=True)
                    last.then_inc(s_sp, 1)

                def turn_b():
                    pe.wait_ge(s_bb, l + 1)
                    for i in range(4):
                        last = pe.transpose(PS[:, 6, P * i:P * i + P], scr[:, 512 + P * i:512 + P * i + P], ident)
                    last.then_inc(s_bTp, 1)

                def bu_product(i):
                    r = slice(32 * (i % 4), 32 * (i % 4) + 32)
                    if i == 0:
                        pe.wait_ge(s_bT, l + 1)
                    else:
                        pe.wait_ge(s_bu, ST * l + i)
                    for c in range(2):
                        last = pe.matmul(PS[:, 6, T * c:T * c + T], bT[r, 2 * c + i // 4, :], uT[r, i // 4, :],
                                         start=True, stop=True)
                    last.then_inc(s_bup, 1)

                def v_part(h):
                    j = h // 2
                    if h == 0:
                        pe.wait_ge(s_win[5], 16 * l + 16)
                    if h % 2 == 0:
                        pe.wait_ge(s_aq, 4 * l + (j + 1))
                    for k in range(4 * (h % 2), 4 * (h % 2) + 4):
                        last = pe.matmul(PS[:, 2 + j, :], hT[:, k, P * j:P * j + P], wchunk(5)[:, k, 0:512],
                                         start=k == 0, stop=k == KD - 1)
                    if h % 2 == 1:
                        last.then_inc(s_pj, 1)

                def y_product(i):
                    m = 32 * (i % 4)
                    pe.wait_ge(s_xr, ST * l + (i + 1))
                    pe.wait_ge(s_xi, ST * l + (i + 1))
                    for c in range(2):
                        last = pe.matmul(PS[m:m + 32, 7, T * (i // 4):T * (i // 4) + T], cT[:, 2 * c + i // 4, m:m + 32],
                                         bu[:, i % 2, c, :], start=c == 0, stop=c == 1)
                    last.then_inc(s_y, 1)

                turn_b()
                decay(0)
                pe.wait_ge(s_qkm, l + 1)
                pe.wait_ge(s_cT, l + 1)
                score(0)
                bu_product(0)
                pe.wait_ge(s_vm, 2 * l + 2)
                for h in range(MH):
                    if h + 1 < MH:
                        decay(h + 1)
                    v_part(h)
                    if h >= 1:
                        y_product(h - 1)
                    bu_product(h + 1)
                    if h == 0:
                        pe.wait_ge(s_aq, 4 * l + 3)
                    pe.wait_ge(s_pm, MH * l + (h + 1))
                    for dst, rhs in ((lambda j: PS[:, 0, T * j + HD * h:T * j + HD * h + HD],
                                      lambda s: vm[:, s, HD * h:HD * h + HD]),
                                     (lambda j: PS[:, 5, 384 + MH * j + h:385 + MH * j + h], lambda s: ones[:, 0:1])):
                        pe.matmul(dst(0), pm[:, 0:P], rhs(0), start=True, stop=True)
                        pe.matmul(dst(1), pm[:, P:T], rhs(0), start=True, stop=False)
                        last = pe.matmul(dst(1), pm[:, T:T + P], rhs(1), start=False, stop=True)
                    last.then_inc(s_np, 1)
                    if h + 1 < MH:
                        score(h + 1)

                def scores(u):
                    j, w, hs = unit(u)
                    if u >= 2:
                        pe.wait_ge(s_pr, 6 * l + (u - 1))
                    else:
                        pe.wait_ge(s_qT, 4 * l + 4)
                        pe.wait_ge(s_mixm, l + 1)
                    for i, h in enumerate(hs):
                        r = slice(64 * (h % 2), 64 * (h % 2) + 64)
                        pe.matmul(PS[:, u % 2, w * i:w * i + w], qkT[r, 0, h // 2, P * j:P * j + P],
                                  qkT[r, 1, h // 2, 0:w], start=True, stop=False)
                        last = pe.matmul(PS[:, u % 2, w * i + w - P:w * i + w], ident, mqk, start=False, stop=True)
                    last.then_inc(s_as, 1)

                for n in range(4):
                    a, j = n // 2, n % 2
                    pe.wait_ge(s_qkn, 4 * l + (n + 1))
                    if n == 3:
                        pe.wait_ge(s_qT, 4 * l + 1)
                    elif n > 0:
                        pe.wait_ge(s_av, 2 * l + n)
                    for c in range(4):
                        last = pe.transpose(PS[:, QK_BANK[n], P * c:P * c + P], qk[:, j, a, P * c:P * c + P], ident)
                    last.then_inc(s_qTp, 1)
                y_product(3)
                bu_product(5)
                pe.wait_ge(s_hm, l + 1)
                for c in range(2):
                    for j in range(NT):
                        last = pe.transpose(PS[:, 0, T * c + P * j:T * c + P * j + P], qkm[:, j, P * c:P * c + P], ident)
                last.then_inc(s_hmT, 1)
                def turn_probs(u):
                    pe.wait_ge(s_pr, 6 * l + (u + 1))
                    if u >= 2:
                        pe.wait_ge(s_pT, 6 * l + (u - 1))
                    for i in range(4):
                        last = pe.transpose(PS[:, 2 + u % 2, P * i:P * i + P], prob[:, u % 2, P * i:P * i + P], ident)
                    last.then_inc(s_pTp, 1)

                def values(u):
                    j, w, hs = unit(u)
                    pe.wait_ge(s_pT, 6 * l + (u + 1))
                    for i, h in enumerate(hs):
                        for k in range(w // P):
                            last = pe.matmul(PS[:, 4 + j, HD * h:HD * h + HD], probT[:, u % 2, w * i + P * k:w * i + P * k + P],
                                             av[:, k, HD * h:HD * h + HD], start=k == 0, stop=k == w // P - 1)
                    last.then_inc(s_pv, 1)

                scores(0)
                scores(1)
                y_product(4)
                bu_product(6)
                turn_probs(0)
                values(0)
                turn_probs(1)
                values(1)
                scores(2)
                scores(3)
                y_product(5)
                bu_product(7)
                turn_probs(2)
                values(2)
                scores(4)
                y_product(6)
                turn_probs(3)
                values(3)
                scores(5)
                y_product(7)
                turn_probs(4)
                values(4)
                turn_probs(5)
                values(5)
                pe.wait_ge(s_z, l + 1)
                for co in range(2):
                    for ci in range(2):
                        last = pe.matmul(PS[:, 6, T * co:T * co + T], gluw[:, ci, P * co:P * co + P],
                                         scr[:, T * ci:T * ci + T], start=ci == 0, stop=ci == 1)
                last.then_inc(s_glu, 1)
                pe.wait_ge(s_on, 2 * l + 2)
                for c in range(2):
                    for i in range(2):
                        for j in range(NT):
                            o = T * i + P * j
                            last = pe.transpose(PS[:, 2 + c, o:o + P], qk[:, j, 0, P * (2 * c + i):P * (2 * c + i) + P],
                                                ident)
                    last.then_inc(s_onT, 1)
                def out_part(j, ks):
                    for n2 in range(2):
                        for k in ks:
                            last = pe.matmul(PS[:, 2 * j + n2, :], mixT[:, k, P * j:P * j + P],
                                             wout[:, k, 512 * n2:512 * n2 + 512], start=k == 0, stop=k == KD - 1)
                    return last

                pe.wait_ge(s_mixa, 2 * l + 2)
                pe.wait_ge(s_wo, 16 * l + 16)
                out_part(0, range(6))
                pe.wait_ge(s_ysq, l + 1)
                for c in range(2):
                    last = pe.matmul(PS[:, 7, T * c:T * c + T], cst[:, C_BLK:C_BLK + P], scr[:, 512 + T * c:512 + T * c + T],
                                     start=True, stop=True)
                last.then_inc(s_ym, 1)
                out_part(1, range(6))
                pe.wait_ge(s_mixs, l + 1)
                for j in range(NT):
                    out_part(j, range(6, KD)).then_inc(s_op, 1)

                turn_xs(l, 1)
                for j in range(NT):
                    for k in range(KD):
                        last = pe.matmul(PS[:, 0, 64 * j:64 * j + 36], hT[:, k, P * j:P * j + P], rw[:, k, :],
                                         start=k == 0, stop=k == KD - 1)
                last.then_inc(s_rp, 1)
                pe.wait_ge(s_mk, l + 1)
                bef = cst[:, C_BEFORE:C_BEFORE + P]
                pe.matmul(PS[:, 1, 0:NE], bef, mks[:, 0, :], start=True, stop=True)
                pe.matmul(PS[:, 1, NE:2 * NE], ones, mks[:, 0, :], start=True, stop=False)
                pe.matmul(PS[:, 1, NE:2 * NE], bef, mks[:, 1, :], start=False, stop=True)
                pe.matmul(PS[:, 1, 2 * NE:3 * NE], ones, mks[:, 0, :], start=True, stop=False)
                pe.matmul(PS[:, 1, 2 * NE:3 * NE], ones, mks[:, 1, :], start=False, stop=True).then_inc(s_rk, 1)
                pe.wait_ge(s_eu, l + 1)
                pe.matmul(PS[0:1, 1, P:P + MAXU], euc, ident[:, 0:MAXU], start=True, stop=True).then_inc(s_eup, 1)

                arrived, weight, used = group_arrived, group_weight, group_used
                wait_apart(pe, s_ctl, l + 1)
                with pe.Fori(0, NG) as g:
                    slots(G, l * NG + g, EG)
                arrived, weight, used = unit_arrived, unit_weight, unit_used
                n_u = pe.value_load(ctl[0:1, 0:1], min_val=1, max_val=MAXU - 1)
                u_0 = pe.value_load(ctl[0:1, 1:2], min_val=0, max_val=L * (MAXU - 1))
                with pe.Fori(0, n_u) as u:
                    slots(U, u_0 + u, 1)


_INS = ["x", "norm1_g", "w_in", "m_bias_i", "m_bias_f", "m_conv_w", "m_conv_b", "m_out_g", "a_q_g", "a_k_g", "a_out_g",
        "s_a_re", "s_a_im", "s_b_re", "s_b_im", "s_c_re", "s_c_im", "s_d", "s_log_dt", "s_glu_w", "s_glu_b", "s_out_g",
        "w_out", "norm2_g", "r_group_w", "r_group_b", "r_expert_w", "r_expert_b", "e_w_gate", "e_w_up", "e_w_down"]


def kernel(**inputs):
    import numpy as _np
    import concourse.bacc as _bacc
    from concourse import mybir as _mybir
    from concourse.bass_utils import run_bass_kernel_spmd as _run

    nc = _bacc.Bacc("TRN2", target_bir_lowering=False, num_devices=1)
    arrays = {"in_consts_dram": constants()}
    for name in _INS:
        arrays[f"in_{name}_dram"] = _np.ascontiguousarray(inputs[name])
    args = [nc.dram_tensor(name, a.shape, _mybir.dt.from_np(a.dtype), kind="ExternalInput").ap()
            for name, a in arrays.items()]
    out = nc.dram_tensor("out_0_dram", (1, T, D), _mybir.dt.float32, kind="ExternalOutput").ap()
    build(nc, out, *args)
    r = _run(nc, [arrays], core_ids=[0])
    return r.results[0]["out_0_dram"]
```
